# Optimizing a Trainium2 kernel written in Bass

```python
import math
import jax, jax.numpy as jnp
from jax import lax
import numpy as np

D_MODEL = 1024
BATCH = 1
SEQ = 256
DEPTH = 2

MEM_LEN = 256
MIX_WIDTH = D_MODEL
SSM_WIDTH = D_MODEL // 4
SSM_GROUP = 16
SSM_GROUPS = SSM_WIDTH // SSM_GROUP
SSM_STATE = 64
SSM_DT_MIN = 1e-3
SSM_DT_MAX = 1e-1
RET_HEADS = 4
RET_HEAD_DIM = D_MODEL // 16
RET_WIDTH = RET_HEADS * RET_HEAD_DIM
RET_CHUNK = 128
ROPE_BASE = 10000.0
SB_HEADS = 8
SB_HEAD_DIM = D_MODEL // 16
SB_WIDTH = SB_HEADS * SB_HEAD_DIM
SB_BLOCK = 128
IN_COLS = SSM_WIDTH + 4 * RET_WIDTH + 3 * SB_WIDTH
CROSS_HEADS = 4
CROSS_HEAD_DIM = D_MODEL // CROSS_HEADS
D_FF = ((8 * D_MODEL // 3 + 255) // 256) * 256
N_EXPERTS = 8
TOP_K = 2
N_DENSE = (DEPTH + 1) // 2
N_MOE = DEPTH // 2
NORM_EPS = 1e-6
GN_EPS = 1e-6

kernel_name = "hybrid_s5_retention_stickbreak_moe"

F32 = jnp.float32

def rms_norm(x, w):
    xf = x.astype(F32)
    y = xf * lax.rsqrt(jnp.mean(xf * xf, axis=-1, keepdims=True) + NORM_EPS)
    return (y * w.astype(F32)).astype(x.dtype)

def _complex_linear_combine(e1, e2):
    a1r, a1i, b1r, b1i = e1
    a2r, a2i, b2r, b2i = e2
    ar = a1r * a2r - a1i * a2i
    ai = a1r * a2i + a1i * a2r
    br = a2r * b1r - a2i * b1i + b2r
    bi = a2r * b1i + a2i * b1r + b2i
    return (ar, ai, br, bi)

def s5_mixer(u, lam_re, lam_im, b_re, b_im, c_re, c_im, d_skip, log_dt, w_glu):
    dtype = u.dtype
    bsz, seq, _ = u.shape
    uf = u.astype(F32)
    ug = uf.reshape(bsz, seq, SSM_GROUPS, SSM_GROUP)
    lr = lam_re.astype(F32)
    li = lam_im.astype(F32)
    dt = jnp.exp(log_dt.astype(F32))[:, None]
    mag = jnp.exp(lr * dt)
    a_re = mag * jnp.cos(li * dt)
    a_im = mag * jnp.sin(li * dt)
    denom = lr * lr + li * li
    nr = a_re - 1.0
    z_re = (nr * lr + a_im * li) / denom
    z_im = (a_im * lr - nr * li) / denom
    br = b_re.astype(F32)
    bi = b_im.astype(F32)
    bb_re = z_re[..., None] * br - z_im[..., None] * bi
    bb_im = z_re[..., None] * bi + z_im[..., None] * br
    bu_re = jnp.einsum('bsgh,gph->bsgp', ug, bb_re)
    bu_im = jnp.einsum('bsgh,gph->bsgp', ug, bb_im)
    a_re_s = jnp.broadcast_to(a_re, (1, seq) + a_re.shape)
    a_im_s = jnp.broadcast_to(a_im, (1, seq) + a_im.shape)
    _, _, x_re, x_im = lax.associative_scan(
        _complex_linear_combine, (a_re_s, a_im_s, bu_re, bu_im), axis=1)
    y = (jnp.einsum('bsgp,ghp->bsgh', x_re, c_re.astype(F32))
         - jnp.einsum('bsgp,ghp->bsgh', x_im, c_im.astype(F32)))
    y = y.reshape(bsz, seq, SSM_WIDTH) + d_skip.astype(F32) * uf
    g = jax.nn.gelu(y)
    out = g * jax.nn.sigmoid(g @ w_glu.astype(F32))
    return out.astype(dtype)

def rotary(x, pos):
    half = x.shape[-1] // 2
    inv_freq = ROPE_BASE ** (-jnp.arange(half, dtype=F32) / half)
    ang = (pos[:, None] * inv_freq[None, :])[None, :, None, :]
    cos, sin = jnp.cos(ang), jnp.sin(ang)
    x1, x2 = x[..., :half], x[..., half:]
    return jnp.concatenate([x1 * cos - x2 * sin, x1 * sin + x2 * cos], axis=-1)

def retention_mixer(q, k, v, g, gn_w):
    dtype = q.dtype
    bsz, seq, _ = q.shape
    H, dh = RET_HEADS, RET_HEAD_DIM
    pos = jnp.arange(seq, dtype=F32)
    qh = rotary(q.reshape(bsz, seq, H, dh).astype(F32), pos)
    kh = rotary(k.reshape(bsz, seq, H, dh).astype(F32), pos) * (dh ** -0.5)
    vh = v.reshape(bsz, seq, H, dh).astype(F32)
    n_chunks = seq // RET_CHUNK

    def to_chunks(t):
        return t.reshape(bsz, n_chunks, RET_CHUNK, H, dh).transpose(1, 0, 3, 2, 4)

    log_gamma = jnp.log1p(-(2.0 ** (-5.0 - jnp.arange(H, dtype=F32))))
    idx = jnp.arange(RET_CHUNK, dtype=F32)
    rel = idx[:, None] - idx[None, :]
    intra = jnp.where(rel >= 0,
                      jnp.exp(log_gamma[:, None, None] * jnp.maximum(rel, 0.0)),
                      0.0)
    xi = jnp.exp(log_gamma[:, None] * (idx + 1.0))[..., None]
    zeta = jnp.exp(log_gamma[:, None] * (RET_CHUNK - 1.0 - idx))[..., None]
    chunk_decay = jnp.exp(log_gamma * RET_CHUNK)[:, None, None]

    def step(state, qkv):
        qc, kc, vc = qkv
        scores = jnp.einsum('bhnd,bhmd->bhnm', qc, kc) * intra
        out = (jnp.einsum('bhnm,bhme->bhne', scores, vc)
               + jnp.einsum('bhnd,bhde->bhne', qc, state) * xi)
        state = chunk_decay * state + jnp.einsum('bhmd,bhme->bhde', kc * zeta, vc)
        return state, out

    state0 = jnp.zeros((bsz, H, dh, dh), F32)
    _, o = lax.scan(step, state0, (to_chunks(qh), to_chunks(kh), to_chunks(vh)))
    o = o.transpose(1, 0, 3, 2, 4).reshape(bsz, seq, H, dh)
    mu = jnp.mean(o, axis=-1, keepdims=True)
    var = jnp.mean(jnp.square(o - mu), axis=-1, keepdims=True)
    o = ((o - mu) * lax.rsqrt(var + GN_EPS)).reshape(bsz, seq, RET_WIDTH) * gn_w.astype(F32)
    out = jax.nn.silu(g.astype(F32)) * o
    return out.astype(dtype)

def stick_breaking_mixer(q, k, v):
    dtype = q.dtype
    bsz, seq, _ = q.shape
    H, dh = SB_HEADS, SB_HEAD_DIM
    qh = q.reshape(bsz, seq, H, dh).transpose(0, 2, 1, 3).astype(F32) * (dh ** -0.5)
    kh = k.reshape(bsz, seq, H, dh).transpose(0, 2, 1, 3).astype(F32)
    vh = v.reshape(bsz, seq, H, dh).transpose(0, 2, 1, 3).astype(F32)
    n_blocks = seq // SB_BLOCK
    q_blocks = qh.reshape(bsz, H, n_blocks, SB_BLOCK, dh).transpose(2, 0, 1, 3, 4)
    starts = jnp.arange(n_blocks, dtype=jnp.int32) * SB_BLOCK
    k_pos = jnp.arange(seq, dtype=jnp.int32)

    def block(args):
        qb, t0 = args
        z = jnp.einsum('bhqd,bhkd->bhqk', qb, kh)
        q_pos = t0 + jnp.arange(SB_BLOCK, dtype=jnp.int32)
        mask = k_pos[None, :] < q_pos[:, None]
        log_fail = jnp.where(mask, jax.nn.log_sigmoid(-z), 0.0)
        after = lax.cumsum(log_fail, axis=3, reverse=True) - log_fail
        w = jnp.where(mask, jnp.exp(jax.nn.log_sigmoid(z) + after), 0.0)
        return jnp.einsum('bhqk,bhkd->bhqd', w, vh)

    o = lax.map(block, (q_blocks, starts))
    o = o.transpose(1, 0, 3, 2, 4).reshape(bsz, seq, SB_WIDTH)
    return o.astype(dtype)

def cross_attention(h, mem_n, w_q, w_kv, w_o):
    bsz, seq, _ = h.shape
    m = mem_n.shape[1]
    q = (h @ w_q).reshape(bsz, seq, CROSS_HEADS, CROSS_HEAD_DIM)
    kv = (mem_n @ w_kv).reshape(bsz, m, 2, CROSS_HEADS, CROSS_HEAD_DIM)
    k, v = kv[:, :, 0], kv[:, :, 1]
    s = jnp.einsum('bshd,bmhd->bhsm', q, k).astype(F32) * (CROSS_HEAD_DIM ** -0.5)
    p = jax.nn.softmax(s, axis=-1).astype(v.dtype)
    o = jnp.einsum('bhsm,bmhd->bshd', p, v).reshape(bsz, seq, D_MODEL)
    return o @ w_o

def swiglu(x, w_gu, w_down):
    gate, up = jnp.split(x @ w_gu, 2, axis=-1)
    return (jax.nn.silu(gate) * up) @ w_down

def moe_swiglu(x, w_router, w_gu, w_down):
    bsz, seq, d = x.shape
    t = x.reshape(bsz * seq, d)
    logits = (t @ w_router).astype(F32)
    top_logits, top_idx = lax.top_k(logits, TOP_K)
    top_w = jax.nn.softmax(top_logits, axis=-1)
    gates = jnp.sum(jax.nn.one_hot(top_idx, N_EXPERTS, dtype=F32) * top_w[..., None], axis=1)
    out = jnp.zeros_like(t)
    for e in range(N_EXPERTS):
        out = out + gates[:, e:e + 1].astype(t.dtype) * swiglu(t, w_gu[e], w_down[e])
    return out.reshape(bsz, seq, d)

def setup_inputs(seed: int = 0) -> dict:
    key = jax.random.key(seed)
    ks = iter(jax.random.split(key, 32))

    def normal(shape, scale):
        return jax.random.normal(next(ks), shape, F32) * scale

    def gain(shape):
        return 1.0 + normal(shape, 0.02)

    n_idx = jnp.arange(SSM_STATE, dtype=F32)
    lam_re = -0.5 + normal((DEPTH, SSM_GROUPS, SSM_STATE), 0.005)
    lam_im = math.pi * n_idx[None, None, :] + normal((DEPTH, SSM_GROUPS, SSM_STATE), 0.005)
    log_dt = jax.random.uniform(next(ks), (DEPTH, SSM_GROUPS), F32,
                                math.log(SSM_DT_MIN), math.log(SSM_DT_MAX))
    return {
        "x": normal((BATCH, SEQ, D_MODEL), 1.0),
        "mem": normal((BATCH, MEM_LEN, D_MODEL), 1.0),
        "mix_norm_w": gain((DEPTH, D_MODEL)),
        "w_in": normal((DEPTH, D_MODEL, IN_COLS), D_MODEL ** -0.5),
        "ssm_lambda_re": lam_re,
        "ssm_lambda_im": lam_im,
        "ssm_b_re": normal((DEPTH, SSM_GROUPS, SSM_STATE, SSM_GROUP), (2 * SSM_GROUP) ** -0.5),
        "ssm_b_im": normal((DEPTH, SSM_GROUPS, SSM_STATE, SSM_GROUP), (2 * SSM_GROUP) ** -0.5),
        "ssm_c_re": normal((DEPTH, SSM_GROUPS, SSM_GROUP, SSM_STATE), SSM_STATE ** -0.5),
        "ssm_c_im": normal((DEPTH, SSM_GROUPS, SSM_GROUP, SSM_STATE), SSM_STATE ** -0.5),
        "ssm_d": normal((DEPTH, SSM_WIDTH), 1.0),
        "ssm_log_dt": log_dt,
        "ssm_w_glu": normal((DEPTH, SSM_WIDTH, SSM_WIDTH), SSM_WIDTH ** -0.5),
        "mix_out_gain": gain((DEPTH, MIX_WIDTH)),
        "w_out": normal((DEPTH, MIX_WIDTH, D_MODEL), MIX_WIDTH ** -0.5),
        "cross_norm_w": gain((DEPTH, D_MODEL)),
        "mem_norm_w": gain((D_MODEL,)),
        "w_cross_q": normal((DEPTH, D_MODEL, D_MODEL), D_MODEL ** -0.5),
        "w_cross_kv": normal((DEPTH, D_MODEL, 2 * D_MODEL), D_MODEL ** -0.5),
        "w_cross_o": normal((DEPTH, D_MODEL, D_MODEL), D_MODEL ** -0.5),
        "ffn_norm_w": gain((DEPTH, D_MODEL)),
        "w_dense_gu": normal((N_DENSE, D_MODEL, 2 * D_FF), D_MODEL ** -0.5),
        "w_dense_down": normal((N_DENSE, D_FF, D_MODEL), D_FF ** -0.5),
        "w_router": normal((N_MOE, D_MODEL, N_EXPERTS), D_MODEL ** -0.5),
        "w_expert_gu": normal((N_MOE, N_EXPERTS, D_MODEL, 2 * D_FF), D_MODEL ** -0.5),
        "w_expert_down": normal((N_MOE, N_EXPERTS, D_FF, D_MODEL), D_FF ** -0.5),
        "final_norm_w": gain((D_MODEL,)),
    }

def reference(x, mem, mix_norm_w, w_in, ssm_lambda_re, ssm_lambda_im, ssm_b_re, ssm_b_im,
              ssm_c_re, ssm_c_im, ssm_d, ssm_log_dt, ssm_w_glu, mix_out_gain, w_out,
              cross_norm_w, mem_norm_w, w_cross_q, w_cross_kv, w_cross_o, ffn_norm_w,
              w_dense_gu, w_dense_down, w_router, w_expert_gu, w_expert_down, final_norm_w):
    o_ret = SSM_WIDTH
    o_sb = SSM_WIDTH + 4 * RET_WIDTH
    mem_n = rms_norm(mem, mem_norm_w)
    h = x
    for i in range(DEPTH):
        proj = rms_norm(h, mix_norm_w[i]) @ w_in[i]
        u_ssm = proj[..., :o_ret]
        r_q = proj[..., o_ret:o_ret + RET_WIDTH]
        r_k = proj[..., o_ret + RET_WIDTH:o_ret + 2 * RET_WIDTH]
        r_v = proj[..., o_ret + 2 * RET_WIDTH:o_ret + 3 * RET_WIDTH]
        r_g = proj[..., o_ret + 3 * RET_WIDTH:o_sb]
        s_q = proj[..., o_sb:o_sb + SB_WIDTH]
        s_k = proj[..., o_sb + SB_WIDTH:o_sb + 2 * SB_WIDTH]
        s_v = proj[..., o_sb + 2 * SB_WIDTH:o_sb + 3 * SB_WIDTH]
        gain_i = mix_out_gain[i]
        y_a = s5_mixer(u_ssm, ssm_lambda_re[i], ssm_lambda_im[i], ssm_b_re[i], ssm_b_im[i],
                       ssm_c_re[i], ssm_c_im[i], ssm_d[i], ssm_log_dt[i], ssm_w_glu[i])
        y_b = retention_mixer(r_q, r_k, r_v, r_g, gain_i[SSM_WIDTH:SSM_WIDTH + RET_WIDTH])
        y_c = stick_breaking_mixer(s_q, s_k, s_v)
        y = jnp.concatenate([
            rms_norm(y_a, gain_i[:SSM_WIDTH]),
            y_b,
            rms_norm(y_c, gain_i[SSM_WIDTH + RET_WIDTH:]),
        ], axis=-1)
        h = h + y @ w_out[i]
        h = h + cross_attention(rms_norm(h, cross_norm_w[i]), mem_n,
                                w_cross_q[i], w_cross_kv[i], w_cross_o[i])
        hn = rms_norm(h, ffn_norm_w[i])
        if i % 2 == 0:
            h = h + swiglu(hn, w_dense_gu[i // 2], w_dense_down[i // 2])
        else:
            h = h + moe_swiglu(hn, w_router[i // 2], w_expert_gu[i // 2], w_expert_down[i // 2])
    return rms_norm(h, final_norm_w)


_drawn_inputs = setup_inputs


def setup_inputs(seed=0):
    import zlib

    import numpy as np

    out = dict(_drawn_inputs(seed))
    spreads = {}
    factors = {'ssm_lambda_re': 64.0,
     'cross_norm_w': 7.214,
     'mem_norm_w': 5.826,
     'final_norm_w': 7.833,
     'ffn_norm_w': 3.97}
    for name, (base, spread) in spreads.items():
        noise = np.random.default_rng([zlib.crc32(name.encode()), seed]).standard_normal(out[name].shape)
        drawn = base * np.exp(spread * noise) if base else spread * noise
        out[name] = __import__('jax').numpy.asarray(drawn.astype(out[name].dtype))
    for name, factor in factors.items():
        out[name] = (out[name] * factor).astype(out[name].dtype)
    return out
```

```python
import math
from contextlib import ExitStack

import numpy as np

import concourse.bass as bass
from concourse import mybir

F32 = mybir.dt.float32
I32 = mybir.dt.int32
ACT = mybir.ActivationFunctionType
ALU = mybir.AluOpType
AX_X = mybir.AxisListType.X

P = 128
D = 1024
S = 256
DEPTH = 2
KC = D // P
TT = S // P
EPS = 1e-6
SSM_W = 256
NT = 8
RH = 4
SH = 8
DH = 64
CH = 4
F = 2816
NJ = F // 256
NE = 8
SLOTS = 11
JOBS_E = 3 * NJ
SLOT = 2048
ROUND = 128
MASKED = -30000.0
TWO_PI_HI = 6.28125
TWO_PI_LO = 2 * math.pi - 6.28125
ROUNDER = 12582912.0

CONST = {}
_at = 0
for _name, _w in (("ident", 128), ("tri_ge", 128), ("ones", 128), ("tri_lt", 128), ("iota", 128),
                  ("group_mask", 128), ("neg_mask", 384), ("mask_bias", 384), ("decay", RH * 256),
                  ("rope_cos", 128), ("rope_sin", 128), ("first_key", 8), ("half", 128)):
    CONST[_name] = (_at, _at + _w)
    _at += _w
CONST_W = _at

ROW = {}
_at = 0
for _l in range(DEPTH):
    for _name, _w in (("lam_re", 8), ("lam_im", 8)):
        ROW[_name, _l] = _at
        _at += _w
for _l in range(DEPTH):
    for _name, _w in (("mix_norm", 8), ("cross_norm", 8), ("ffn_norm", 8), ("gain", 8), ("ssm_d", 2)):
        ROW[_name, _l] = _at
        _at += _w
ROW["mem_norm", 0] = _at
_at += 8
ROWS = _at


def constants():
    c = np.zeros((P, CONST_W), np.float32)

    def put(name, a):
        c[:, CONST[name][0]:CONST[name][1]] = a.reshape(P, -1)

    p = np.arange(P)
    put("ident", np.eye(P))
    put("tri_ge", (p[:, None] >= p[None, :]) * 1.0)
    put("ones", np.ones((P, P)))
    put("tri_lt", (p[:, None] < p[None, :]) * 1.0)
    put("iota", np.tile(p, (P, 1)))
    put("group_mask", ((p[None, :] // 16) % 2 == (p[:, None] >= 64)) * 1.0)
    q = np.concatenate([np.arange(256), np.arange(128)])
    strict = p[:, None] < q[None, :]
    put("neg_mask", -1.0 * strict)
    put("mask_bias", np.where(strict, 0.0, MASKED))
    lg = np.log1p(-(2.0 ** (-5.0 - np.arange(RH, dtype=np.float64))))
    rel = np.arange(256)[None, :] - p[:, None]
    put("decay", np.where(rel[:, None] >= 0, np.exp(lg[None, :, None] * np.maximum(rel, 0)[:, None]), 0.0))
    inv = (10000.0 ** (-np.arange(32, dtype=np.float32) / np.float32(32))).astype(np.float32)
    ang = (np.arange(S, dtype=np.float32)[:, None] * inv[None, :]).astype(np.float32).reshape(TT, P, 32)
    ang = ang.transpose(1, 0, 2).astype(np.float64)
    scale = np.array([1.0, DH ** -0.5])[None, None, :, None]
    put("rope_cos", np.cos(ang)[:, :, None] * scale)
    put("rope_sin", np.sin(ang)[:, :, None] * scale)
    put("first_key", np.tile(8.0 - np.arange(8), (P, 1)))
    put("half", (p[:, None] == p[None, :] // 64) * 1.0)
    return c


def plan_jobs():
    jobs = []

    def full(name, l, cb):
        jobs.extend([(name, l, cb, 0), (name, l, cb, 1)])

    def swiglu(name):
        out = []
        for step in range(NJ + 2):
            if step < NJ:
                out += [(name + "_gu", step, 0), (name + "_gu", step, 1)]
            if step >= 2:
                out.append((name + "_down", step - 2))
        return out

    for l in range(DEPTH):
        jobs.append(("in_u", l, 0, 0))
        for cb in ("rqk", "sq", "sk", "rvg", "sv"):
            full("in", l, cb)
        for cb in range(4):
            full("kv", l, cb)
        for name in ("out", "q", "o"):
            for cb in range(2):
                full(name, l, cb)
        if l == 0:
            jobs += swiglu("dense")
    return jobs, swiglu("expert")


def plan_banks():
    uses, count = {}, [0] * 8

    def use(bank, *key):
        uses[key] = (bank, count[bank])
        count[bank] += 1

    turn = [0]

    def rot(*key, among=range(8)):
        use(among[turn[0] % len(among)], *key)
        turn[0] += 1

    rot("cols")
    for i in range(4):
        rot("normT", "mem", 0, i)
    for l in range(DEPTH):
        for i in range(4):
            rot("normT", l, "mix", i)
        rot("u", l)
        rot("rqk", l, 0)
        rot("rqk", l, 1)
        rot("BT", l)
        rot("CT", l)
        for i in range(NT):
            rot("bu", l, i)
        for name in ("sq", "sk"):
            rot(name, l, 0)
            rot(name, l, 1)
        for name in ("rvg", "sv"):
            rot(name, l, 0)
            rot(name, l, 1)
        rot("rT", l, 0)
        rot("rT", l, 1)
        use(7, "ro", l)
        for h in range(RH):
            use(h % 2, "rs", l, h)
        use(2, "ybT", l)
        for h in range(SH + 2):
            if h < SH:
                use(3 + h % 3, "sz", l, h)
            if 1 <= h <= SH:
                use(3 + (h - 1) % 3, "sc", l, h - 1)
            if h >= 2 and h % 4 == 2 and (h - 2) // 4 < 2:
                use(6 + (h - 2) // 4, "so", l, (h - 2) // 4)
        turn[0] = 0
        for i in range(4):
            rot("kT", l, i)
        for cb in range(2):
            rot("v", l, cb, 0)
            rot("v", l, cb, 1)
        rot("y", l)
        rot("glu", l)
        rot("ssa", l)
        rot("ssc", l)
        for n in range(2):
            rot("out", l, n, 0)
            rot("out", l, n, 1)
        for i in range(4):
            rot("normT", l, "cross", i)
        for i in range(4):
            rot("q", l, i)
        for h in range(CH):
            rot("cs", l, h)
            if h:
                rot("cp", l, h - 1)
                rot("co", l, h - 1)
        rot("cp", l, CH - 1)
        rot("co", l, CH - 1)
        for n in range(2):
            rot("o", l, n, 0)
            rot("o", l, n, 1)
        for i in range(4):
            rot("normT", l, "ffn", i)
        if l == 0:
            for s in range(NJ + 2):
                if s < NJ:
                    use(4, "gu", s, 0)
                    use(5, "gu", s, 1)
                if 1 <= s <= NJ:
                    use(6, "hT", s - 1, 0)
                    use(7, "hT", s - 1, 1)
            for b in range(4):
                use(b, "down", b)
        else:
            rot("logits")
            rot("rank")
            for i in range(4):
                rot("scT", 0, i)
    before = list(count)

    def expert(r):
        use(6, "xg", r, 0)
        use(7, "xg", r, 1)
        for s in range(NJ + 2):
            if s < NJ:
                use(2 + s % 2, "egu", r, s)
            if 1 <= s <= NJ:
                use(4 + (s - 1) % 2, "ehT", r, s - 1)
        use(0, "ey", r, 0)
        use(1, "ey", r, 1)
        for i in range(4):
            use((6, 7, 2, 3)[i], "eo", r, i)

    expert(0)
    per_expert = [count[b] - before[b] for b in range(8)]
    for b in range(8):
        count[b] = before[b] + NE * per_expert[b]
    turn[0] = 0
    for i in range(4):
        rot("scT", 1, i)
    expert(1)
    return uses, per_expert


N_ROW_LOADS = 8 * DEPTH + 2
N_SSM_LOADS = 7
IN_COLS = {"u": 0, "rqk": 256, "rvg": 768, "sq": 1280, "sk": 1792, "sv": 2304}


def trunk(nc, a, out):
    jobs, expert_jobs = plan_jobs()
    job_no = {k: n for n, k in enumerate(jobs)}
    ejob_no = {k: n for n, k in enumerate(expert_jobs)}
    BASE = len(jobs)
    uses, per_expert = plan_banks()

    with ExitStack() as ctx:
        def sb(name, *shape, dt=F32):
            return ctx.enter_context(nc.sbuf_tensor(name, [P, *shape], dt))

        def sem(name):
            return ctx.enter_context(nc.semaphore(name))

        ps = ctx.enter_context(nc.psum_tensor("ps", [P, 8, 512], F32))
        ring = sb("ring", SLOTS, SLOT)
        h = sb("h", TT, D)
        hs = sb("hs", TT, D)
        xT = sb("xT", KC, S)
        yT = sb("yT", KC, S)
        memT = sb("memT", KC, S)
        ckv = sb("ckv", 2, 2048)
        consts = sb("consts", CONST_W)
        rows_in = sb("rows_in", P)
        ldt = sb("ldt", DEPTH, NT)
        cols = sb("cols", P + DEPTH * NT)
        braw = sb("braw", 2, NT, 16)
        craw = sb("craw", 2, 2, 2, 64)
        wglu = sb("wglu", 2, 256)
        wrt = sb("wrt", KC, NE)
        sp = sb("sp", 20, DEPTH * NT)
        stat = sb("stat", 64)
        flag = sb("flag", 1, dt=I32)
        rot_tab = sb("rot_tab", 2, NT, S)
        zone_b = sb("zone_b", NT, 2, S)
        zone_s = sb("zone_s", 6144)
        ptmp = sb("ptmp", 2, S)
        eps = sb("eps", 1)
        cstat = sb("cstat", 4)

        def c(name):
            return consts[:, CONST[name][0]:CONST[name][1]]

        ident, ones = c("ident"), c("ones")

        def col(name, l, i):
            r = ROW[name, l] + i
            return cols[:, r:r + 1]

        kT = ckv[:, 0, :].rearrange("p (c s) -> p c s", c=KC)
        vr = ckv[:, 1, :].rearrange("p (t d) -> p t d", t=TT)
        rqkT = ckv[:, 0, 0:1024].rearrange("p (c s) -> p c s", c=4)
        rvg = ckv[:, 0, 1024:2048].rearrange("p (t d) -> p t d", t=TT)
        rsc = ckv[:, 1, 0:768].rearrange("p (b s) -> p b s", b=2)
        ro = ckv[:, 1, 768:1280].rearrange("p (t d) -> p t d", t=TT)
        ro2 = ckv[:, 1, 1280:1792].rearrange("p (t d) -> p t d", t=TT)
        rqk = yT[:, 4:8, :].rearrange("p (t q) s -> p t (q s)", t=TT)
        rtmp = yT[:, 0:2, :].rearrange("p (x q) s -> p x (q s)", x=2)
        sqT = zone_s[:, 0:1024].rearrange("p (c s) -> p c s", c=4)
        skT = zone_s[:, 1024:2048].rearrange("p (c s) -> p c s", c=4)
        sv = zone_s[:, 2048:3072].rearrange("p (t d) -> p t d", t=TT)
        sa = zone_s[:, 3072:3840].rearrange("p (b s) -> p b s", b=2)
        slf = xT[:, 0:3, :].rearrange("p c s -> p (c s)").rearrange("p (b s) -> p b s", b=2)
        sw = xT[:, 3:6, :].rearrange("p c s -> p (c s)").rearrange("p (b s) -> p b s", b=2)
        uT = zone_s[:, 3840:4352].rearrange("p (c s) -> p c s", c=2)
        bb = zone_s[:, 4352:4864].rearrange("p (r i x) -> p r i x", r=2, i=NT)
        BT = zone_s[:, 4864:5376].rearrange("p (f r s) -> p f r s", f=2, r=2)
        CT = zone_s[:, 5376:5888].rearrange("p (f r s) -> p f r s", f=2, r=2)
        bbt = zone_s[:, 5888:6144].rearrange("p (r i x) -> p r i x", r=2, i=NT)
        yin = hs[:, 0, :].rearrange("p (r i s) -> p r i s", r=2, i=2)
        ysc = hs[:, 1, :].rearrange("p (r i s) -> p r i s", r=2, i=2)
        vtmp = yT[:, 2:4, :]
        rot_tmp = ckv[:, 1, :].rearrange("p (x i s) -> p x i s", x=2, i=NT)
        gT = zone_b[:, 0]
        glu_s = zone_b[:, 1]
        sq_a = zone_b[:, 2]
        sq_c = zone_b[:, 4:6].rearrange("p i r s -> p (i r) s")
        rstd_a = zone_b[:, 3, 0]
        rstd_c = zone_b[:, 3, 1]
        cqT = zone_b[:, 0:4].rearrange("p i r s -> p (i r) s")
        cp = zone_b[:, 4:6].rearrange("p i r s -> p i r s")
        cpT = zone_b[:, 6:8]
        sg = zone_s[:, 0:512].rearrange("p (b s) -> p b s", b=2)
        hh = zone_s[:, 512:1536].rearrange("p (b t s) -> p b t s", b=2, t=2)
        hT = zone_s[:, 1536:2560].rearrange("p (b k s) -> p b k s", b=2, k=2)
        sel = rot_tab[:, 0].rearrange("p i s -> p (i s)")
        gsel = zone_b[:, 0:4].rearrange("p i r s -> p (i r s)")
        scT = rot_tab[:, 1].rearrange("p i s -> p (i s)")
        xg = zone_s[:, 2560:3584].rearrange("p (c s) -> p c s", c=KC)
        ye = zone_s[:, 3584:4608]
        sc_cur = zone_s[:, 4608:4864]
        rt = zone_s[:, 4864:5888].rearrange("p (n x) -> p n x", n=64)
        fin_w = yT[:, 0:4, :].rearrange("p c s -> p (c s)")
        sqj = yT[:, 4:8, :].rearrange("p c s -> p (c s)")

        landed = [sem(f"slot{s}_landed") for s in range(SLOTS)]
        bank_filled = [sem(f"bank{b}_filled") for b in range(8)]
        bank_free = [sem(f"bank{b}_free") for b in range(8)]
        consts_in, x_in, mem_in, rows_landed, ssm_in, router_in, finw_in, out_done = (
            sem(n) for n in ("consts_in", "x_in", "mem_in", "rows_landed", "ssm_in", "router_in", "finw_in", "out_done"))
        dve_step, act_step, pool_step = sem("dve_step"), sem("act_step"), sem("pool_step")
        names = ("eps_ready rstd_ready hs_ready sp_dt sp_range sp_sin sp_ready bb_ready rot_ready yin_im ysc_ready "
                 "x_re x_im rqk_ready rgn_sq rgn_rstd yb_ready sa_ready slf_ready sw_ready gelu_ready glu_ready sqa_ready "
                 "sqc_ready rstda rstdc ya_T yc_T cs_max cp_exp cp_ready gate_exp gate_in sel_ready gsel_ready mask_ready "
                 "flag_ready sg_ready sc_ready h_final final_ready").split()
        s = {n: sem(n) for n in names}

        def bank(key):
            return ps[:, uses[key][0], :]

        def wait_filled(eng, *key, e=None):
            b, n = uses[key]
            eng.wait_ge(bank_filled[b], n + 1 if e is None else e * per_expert[b] + (n + 1))

        def wait_taken(eng, *key, e=None):
            b, n = uses[key]
            eng.wait_ge(bank_free[b], n + 1 if e is None else e * per_expert[b] + (n + 1))

        def free(ins, *key):
            ins.then_inc(bank_free[uses[key][0]], 1)

        class Chain:

            def __init__(self, eng, sem_, base=0):
                self.eng, self.sem, self.n = eng, sem_, base

            def do(self, ins):
                ins.then_inc(self.sem, 1)
                self.n += 1
                self.settle()

            def settle(self):
                self.eng.wait_ge(self.sem, self.n)

        release = {}
        for l in range(DEPTH):
            release["in_u", l, 0, 0] = ("u", l)
            for n in ("rqk", "rvg", "sv"):
                release["in", l, n, 0] = release["in", l, n, 1] = (n, l, 1)
            for n in ("sq", "sk"):
                release["in", l, n, 0] = release["in", l, n, 1] = (n, l, 1)
            for cb in range(4):
                for k in range(2):
                    release["kv", l, cb, k] = ("kT", l, 2 * cb + 1) if cb < 2 else ("v", l, cb - 2, 1)
            for cb in range(2):
                for k in range(2):
                    release["out", l, cb, k] = ("out", l, cb, 1)
                    release["o", l, cb, k] = ("o", l, cb, 1)
                    release["q", l, cb, k] = ("q", l, 2 * cb + 1)
        for j in range(NJ):
            release["dense_gu", j, 0] = release["dense_gu", j, 1] = ("gu", j, 1)
            release["dense_down", j] = ("hT", j + 1, 1) if j + 1 < NJ else ("down", 3)

        def expert_release(r):
            out = {}
            for j in range(NJ):
                out["expert_gu", j, 0] = out["expert_gu", j, 1] = ("egu", r, j)
                out["expert_down", j] = ("ehT", r, j + 1) if j + 1 < NJ else ("ey", r, 1)
            return out

        def source(job):
            name = job[0]
            if name == "in_u":
                return a["w_in"][job[1], :, 0:256].rearrange("(k p) n -> p k n", p=P)
            if name == "in":
                o = IN_COLS[job[2]]
                w = a["w_in"][job[1], :, o:o + 512]
            elif name == "kv":
                w = a["w_cross_kv"][job[1], :, job[2] * 512:job[2] * 512 + 512]
            elif name in ("out", "q", "o"):
                w = a[{"out": "w_out", "q": "w_cross_q", "o": "w_cross_o"}[name]][job[1], :, job[2] * 512:job[2] * 512 + 512]
            elif name == "dense_gu":
                w = a["w_dense_gu"][0].rearrange("(k p) (g f) -> p k g f", p=P, g=2)
                return w[:, 4 * job[2]:4 * job[2] + 4, :, 256 * job[1]:256 * job[1] + 256]
            elif name == "dense_down":
                return a["w_dense_down"][0, 256 * job[1]:256 * job[1] + 256, :].rearrange("(k p) n -> p k n", p=P)
            w = w.rearrange("(k p) n -> p k n", p=P)
            return w[:, 4 * job[3]:4 * job[3] + 4, :]

        def slot_of(n):
            return ring[:, n % SLOTS, :]

        def start_load(sp_, n, src):
            dst = slot_of(n)
            if len(src.shape) == 4:
                dst = dst.rearrange("p (k g f) -> p k g f", k=4, g=2)
                for g in range(2):
                    sp_.dma_start(dst[:, :, g, :], src[:, :, g, :]).then_inc(landed[n % SLOTS], 16)
            else:
                dst = dst.rearrange("p (k n) -> p k n", k=src.shape[1])
                sp_.dma_start(dst, src).then_inc(landed[n % SLOTS], 16)

        def parts(key):
            return 2 if key[0].endswith("_gu") else 1

        landed_at, total = {}, [0] * SLOTS
        for n, k in enumerate(jobs):
            total[n % SLOTS] += 16 * parts(k)
            landed_at[n] = total[n % SLOTS]
        e_landed, e_total = {}, [0] * SLOTS
        for i, k in enumerate(expert_jobs):
            e_total[(BASE + i) % SLOTS] += 16 * parts(k)
            e_landed[i] = total[(BASE + i) % SLOTS] + e_total[(BASE + i) % SLOTS]

        block = ctx.enter_context(nc.Block())

        @block.sync
        def _(sync):
            sync.dma_start(memT[:, 0:4, :].rearrange("p c s -> p (c s)"), a["mem"][0, 0:128, :]).then_inc(mem_in, 16)
            sync.dma_start(memT[:, 4:8, :].rearrange("p c s -> p (c s)"), a["mem"][0, 128:256, :]).then_inc(mem_in, 16)
            sync.dma_start(consts[:, :], a["consts"]).then_inc(consts_in, 16)
            sync.dma_start(h[:, :, :], a["x"][0].rearrange("(t p) d -> p t d", p=P)).then_inc(x_in, 16)
            for n in range(SLOTS):
                start_load(sync, n, source(jobs[n]))
            for n in range(SLOTS, BASE):
                wait_filled(sync, *release[jobs[n - SLOTS]])
                start_load(sync, n, source(jobs[n]))

            def expert_source(i, e):
                k = expert_jobs[i]
                if k[0] == "expert_gu":
                    w = a["w_expert_gu"][0].rearrange("e (k p) (g f) -> p e k g f", p=P, g=2)
                    w = w[:, e, 4 * k[2]:4 * k[2] + 4, :, 256 * k[1]:256 * k[1] + 256] if isinstance(e, int) else \
                        w[:, bass.ds(e, 1), 4 * k[2]:4 * k[2] + 4, :, 256 * k[1]:256 * k[1] + 256].rearrange("p e k g f -> p (e k) g f")
                    return w
                w = a["w_expert_down"][0].rearrange("e (j k p) n -> p e j k n", p=P, k=2)
                return w[:, e, k[1]] if isinstance(e, int) else \
                    w[:, bass.ds(e, 1), k[1]].rearrange("p e k n -> p (e k) n")

            def expert_round(r):
                rel = expert_release(r)
                for i in range(SLOTS):
                    if r == 0:
                        wait_filled(sync, *release[jobs[BASE - SLOTS + i]])
                    start_load(sync, BASE + i, expert_source(i, 0))
                with sync.Fori(0, NE - 1) as e:
                    for i in range(SLOTS, JOBS_E):
                        wait_filled(sync, *rel[expert_jobs[i - SLOTS]], e=e)
                        start_load(sync, BASE + i, expert_source(i, e))
                    for i in range(SLOTS):
                        wait_filled(sync, *rel[expert_jobs[i + JOBS_E - SLOTS]], e=e)
                        start_load(sync, BASE + i, expert_source(i, e + 1))
                for i in range(SLOTS, JOBS_E):
                    wait_filled(sync, *rel[expert_jobs[i - SLOTS]], e=NE - 1)
                    start_load(sync, BASE + i, expert_source(i, NE - 1))
                wait_filled(sync, "ey", r, 1, e=NE - 1)

            expert_round(0)
            sync.wait_ge(s["flag_ready"], 1)
            more = sync.value_load(flag[0:1, 0:1], min_val=0, max_val=1)
            with sync.If(more):
                expert_round(1)
            sync.wait_ge(s["final_ready"], TT)
            sync.dma_start(out[0].rearrange("(t p) d -> p t d", p=P), hs[:, :, :]).then_inc(out_done, 16)
            sync.wait_ge(out_done, 16)

        @block.tensor
        def _(pe):
            seen = [0] * 8

            def claim(*key, e=None, again=False):
                b, n = uses[key]
                if e is None:
                    assert seen[b] == n, key
                    seen[b] += 1
                    if n:
                        pe.wait_ge(bank_free[b], n)
                else:
                    pe.wait_ge(bank_free[b], e * per_expert[b] + n)
                return ps[:, b, :]

            def done(mm, *key):
                mm.then_inc(bank_filled[uses[key][0]], 1)

            def arrived(key, e=None, r=0):
                if e is None:
                    n = job_no[key]
                    pe.wait_ge(landed[n % SLOTS], landed_at[n])
                    return slot_of(n)
                i = ejob_no[key]
                sl = (BASE + i) % SLOTS
                pe.wait_ge(landed[sl], e * e_total[sl] + (e_landed[i] + r * NE * e_total[sl]))
                return slot_of(BASE + i)

            def transposes_of_rows(l, which, src):
                for i in range(4):
                    bk = claim("normT", l, which, i)
                    for cc in range(2):
                        for t in range(TT):
                            o = cc * 256 + t * P
                            ch = 2 * i + cc
                            mm = nc.tensor.transpose(bk[:, o:o + P], src[:, t, ch * P:(ch + 1) * P], ident)
                    done(mm, "normT", l, which, i)

            def rows_product(keys, lhs, name, l, cb, kc=KC):
                banks = [claim(*k) for k in keys]
                for kh in range(2):
                    w = arrived((name, l, cb, kh)).rearrange("p (k n) -> p k n", k=4)
                    for t in range(TT):
                        for k in range(4):
                            kk = 4 * kh + k
                            mm = nc.tensor.matmul(banks[t], lhs[:, kk, t * P:(t + 1) * P], w[:, k, :],
                                                  start=(kk == 0), stop=(kk == KC - 1))
                        if kh:
                            done(mm, *keys[t])

            def cols_product(keys, rhs, name, l, cb):
                ws = [arrived((name, l, cb, kh)).rearrange("p (k n) -> p k n", k=4) for kh in range(2)]
                for i, key in enumerate(keys):
                    bk = claim(*key)
                    for cc in range(2):
                        m = (2 * i + cc) * P
                        for kk in range(KC):
                            mm = nc.tensor.matmul(bk[:, cc * 256:cc * 256 + 256], ws[kk // 4][:, kk % 4, m:m + P],
                                                  rhs[:, kk, :], start=(kk == 0), stop=(kk == KC - 1))
                    done(mm, *key)

            def all_taken(*keys):
                for k in keys:
                    wait_taken(pe, *k)

            def xT_written(l, which):
                all_taken(*[("normT", l, which, i) for i in range(4)])

            pe.wait_ge(consts_in, 16)
            pe.wait_ge(rows_landed, 16 * N_ROW_LOADS)
            bk = claim("cols")
            nc.tensor.transpose(bk[:, 0:P], rows_in[:, :], ident)
            mm = nc.tensor.matmul(bk[:, P:P + DEPTH * NT], c("half")[0:2, :], ldt[0:2].rearrange("p l i -> p (l i)"),
                                  start=True, stop=True)
            done(mm, "cols")
            pe.wait_ge(s["hs_ready"], 1)
            transposes_of_rows("mem", 0, hs)

            for l in range(DEPTH):
                pe.wait_ge(s["hs_ready"], 2 + 3 * l)
                transposes_of_rows(l, "mix", hs)
                xT_written(l, "mix")
                w = arrived(("in_u", l, 0, 0)).rearrange("p (k n) -> p k n", k=KC)
                bk = claim("u", l)
                for cc in range(2):
                    for k in range(KC):
                        mm = nc.tensor.matmul(bk[:, cc * 256:cc * 256 + 256], w[:, k, cc * P:(cc + 1) * P], xT[:, k, :],
                                              start=(k == 0), stop=(k == KC - 1))
                done(mm, "u", l)
                rows_product([("rqk", l, t) for t in range(TT)], xT, "in", l, "rqk")
                pe.wait_ge(s["bb_ready"], l + 1)
                bk = claim("BT", l)
                for f in range(2):
                    for r in range(2):
                        o = (2 * f + r) * P
                        mm = nc.tensor.transpose(bk[:, o:o + P], bb[:, r, 4 * f:4 * f + 4, :].rearrange("p i x -> p (i x)"), ident)
                done(mm, "BT", l)
                pe.wait_ge(ssm_in, 16 * N_SSM_LOADS * (l + 1))
                bk = claim("CT", l)
                for f in range(2):
                    for r in range(2):
                        o = (2 * f + r) * P
                        mm = nc.tensor.transpose(bk[:, o:o + P], craw[:, f, r].rearrange("p a n -> p (a n)"), ident)
                done(mm, "CT", l)
                all_taken(("u", l), ("BT", l))
                for i in range(NT):
                    bk = claim("bu", l, i)
                    q = 32 * (i % 4)
                    for r in range(2):
                        mm = nc.tensor.matmul(bk[:, 256 * r:256 * r + 256], BT[q:q + 32, i // 4, r, :], uT[q:q + 32, i // 4, :],
                                              start=True, stop=True)
                    done(mm, "bu", l, i)
                cols_product([("sq", l, 0), ("sq", l, 1)], xT, "in", l, "sq")
                cols_product([("sk", l, 0), ("sk", l, 1)], xT, "in", l, "sk")
                rows_product([("rvg", l, t) for t in range(TT)], xT, "in", l, "rvg")
                rows_product([("sv", l, t) for t in range(TT)], xT, "in", l, "sv")
                pe.wait_ge(s["rqk_ready"], l + 1)
                for w_ in range(2):
                    bk = claim("rT", l, w_)
                    for cc in range(2):
                        for t in range(TT):
                            o = cc * 256 + t * P
                            mm = nc.tensor.transpose(bk[:, o:o + P], rqk[:, t, 256 * w_ + cc * P:256 * w_ + (cc + 1) * P], ident)
                    done(mm, "rT", l, w_)
                all_taken(("rT", l, 0), ("rT", l, 1), ("rvg", l, 0), ("rvg", l, 1))
                ob = claim("ro", l)

                def ret_scores(hd):
                    bk = claim("rs", l, hd)
                    p0, cc = DH * (hd % 2), hd // 2
                    nc.tensor.matmul(bk[:, 0:256], rqkT[p0:p0 + DH, 2 + cc, 0:P], rqkT[p0:p0 + DH, cc, :], start=True, stop=True)
                    mm = nc.tensor.matmul(bk[:, 256:384], rqkT[p0:p0 + DH, 2 + cc, P:256], rqkT[p0:p0 + DH, cc, P:256],
                                          start=True, stop=True)
                    done(mm, "rs", l, hd)

                def ret_out(hd):
                    wait_taken(pe, "rs", l, hd)
                    sc, o = rsc[:, hd % 2], DH * hd
                    nc.tensor.matmul(ob[:, o:o + DH], sc[:, 0:P], rvg[:, 0, o:o + DH], start=True, stop=True)
                    nc.tensor.matmul(ob[:, 256 + o:256 + o + DH], sc[:, P:256], rvg[:, 0, o:o + DH], start=True, stop=False)
                    return nc.tensor.matmul(ob[:, 256 + o:256 + o + DH], sc[:, 256:384], rvg[:, 1, o:o + DH],
                                            start=False, stop=True)

                for hd in range(RH):
                    ret_scores(hd)
                    if hd:
                        ret_out(hd - 1)
                done(ret_out(RH - 1), "ro", l)
                all_taken(*[(n, l, i) for n in ("sq", "sk", "sv") for i in range(2)])
                for step in range(SH + 2):
                    if step < SH:
                        hd = step
                        bk = claim("sz", l, hd)
                        p0, cc = DH * (hd % 2), hd // 2
                        nc.tensor.matmul(bk[:, 0:256], skT[p0:p0 + DH, cc, 0:P], sqT[p0:p0 + DH, cc, :], start=True, stop=True,
                                         skip_group_check=True)
                        mm = nc.tensor.matmul(bk[:, 256:384], skT[p0:p0 + DH, cc, P:256], sqT[p0:p0 + DH, cc, P:256],
                                              start=False, stop=True, skip_group_check=True)
                        done(mm, "sz", l, hd)
                    if 1 <= step <= SH:
                        hd = step - 1
                        bk = claim("sc", l, hd)
                        pe.wait_ge(s["slf_ready"], SH * l + hd + 1)
                        lf = slf[:, hd % 2]
                        nc.tensor.matmul(bk[:, 0:256], c("tri_ge"), lf[:, 0:256], start=False, stop=True, skip_group_check=True)
                        nc.tensor.matmul(bk[:, P:256], ones, lf[:, 256:384], start=False, stop=True, skip_group_check=True)
                        mm = nc.tensor.matmul(bk[:, 256:384], c("tri_ge"), lf[:, 256:384], start=False, stop=True,
                                              skip_group_check=True)
                        done(mm, "sc", l, hd)
                    if step >= 2:
                        hd = step - 2
                        if hd % 4 == 0:
                            so = claim("so", l, hd // 4)
                        pe.wait_ge(s["sw_ready"], SH * l + hd + 1)
                        w = sw[:, hd % 2]
                        p0, o = DH * (hd % 2), 256 * (hd // 2 % 2)
                        vv = slice(DH * hd, DH * hd + DH)
                        nc.tensor.matmul(so[p0:p0 + DH, o:o + 256], sv[:, 0, vv], w[:, 0:256], start=True, stop=False,
                                         skip_group_check=True)
                        mm = nc.tensor.matmul(so[p0:p0 + DH, o + P:o + 256], sv[:, 1, vv], w[:, 256:384], start=False, stop=True,
                                              skip_group_check=True)
                        if hd % 4 == 3:
                            done(mm, "so", l, hd // 4)
                pe.wait_ge(s["yb_ready"], l + 1)
                bk = claim("ybT", l)
                for cc in range(2):
                    for t in range(TT):
                        o = cc * 256 + t * P
                        mm = nc.tensor.transpose(bk[:, o:o + P], ro[:, t, cc * P:(cc + 1) * P], ident)
                done(mm, "ybT", l)
                xT_written("mem", 0)
                for cb in range(2):
                    cols_product([("kT", l, 2 * cb), ("kT", l, 2 * cb + 1)], memT, "kv", l, cb)
                for cb in range(2):
                    rows_product([("v", l, cb, t) for t in range(TT)], memT, "kv", l, 2 + cb)
                wait_taken(pe, "CT", l)
                bk = claim("y", l)
                for i in range(NT):
                    if i % 2 == 0:
                        pe.wait_ge(s["x_re"], 4 * l + i // 2 + 1)
                        pe.wait_ge(s["x_im"], 4 * l + i // 2 + 1)
                    q = 32 * (i % 4)
                    for r in range(2):
                        mm = nc.tensor.matmul(bk[q:q + 32, 256 * (i // 4):256 * (i // 4) + 256], CT[:, i // 4, r, q:q + 32],
                                              zone_b[:, i, r, :], start=(r == 0), stop=(r == 1), skip_group_check=True)
                done(mm, "y", l)
                pe.wait_ge(s["gelu_ready"], l + 1)
                bk = claim("glu", l)
                for m in range(2):
                    for k in range(2):
                        mm = nc.tensor.matmul(bk[:, 256 * m:256 * m + 256], wglu[:, k, P * m:P * m + P], gT[:, k, :],
                                              start=(k == 0), stop=(k == 1))
                done(mm, "glu", l)
                for key, ready, sq, n in (("ssa", "sqa_ready", sq_a, 2), ("ssc", "sqc_ready", sq_c, 4)):
                    pe.wait_ge(s[ready], l + 1)
                    bk = claim(key, l)
                    for k in range(n):
                        mm = nc.tensor.matmul(bk[:, 0:256], ones, sq[:, k, :], start=(k == 0), stop=(k == n - 1))
                    done(mm, key, l)
                pe.wait_ge(s["ya_T"], l + 1)
                wait_taken(pe, "ybT", l)
                pe.wait_ge(s["yc_T"], l + 1)
                for cb in range(2):
                    rows_product([("out", l, cb, t) for t in range(TT)], yT, "out", l, cb)

                pe.wait_ge(s["hs_ready"], 3 + 3 * l)
                transposes_of_rows(l, "cross", hs)
                xT_written(l, "cross")
                for cb in range(2):
                    cols_product([("q", l, 2 * cb), ("q", l, 2 * cb + 1)], xT, "q", l, cb)
                all_taken(*[(n, l, i) for n in ("q", "kT") for i in range(4)])
                all_taken(*[("v", l, cb, t) for cb in range(2) for t in range(TT)])

                def cross_scores(hd):
                    bk = claim("cs", l, hd)
                    for t in range(TT):
                        for k in range(2):
                            mm = nc.tensor.matmul(bk[:, 256 * t:256 * t + 256], cqT[:, 2 * hd + k, t * P:(t + 1) * P],
                                                  kT[:, 2 * hd + k, :], start=(k == 0), stop=(k == 1))
                    done(mm, "cs", l, hd)

                def cross_out(hd):
                    pe.wait_ge(s["cp_ready"], CH * l + hd + 1)
                    bk = claim("cp", l, hd)
                    for m in range(2):
                        for t in range(TT):
                            o = 256 * m + t * P
                            mm = nc.tensor.transpose(bk[:, o:o + P], cp[:, hd % 2, t, m * P:(m + 1) * P], ident)
                    done(mm, "cp", l, hd)
                    wait_taken(pe, "cp", l, hd)
                    bk = claim("co", l, hd)
                    for cc in range(2):
                        for m in range(2):
                            ch = (2 * hd + cc) * P
                            mm = nc.tensor.matmul(bk[:, 256 * cc:256 * cc + 256], vr[:, m, ch:ch + P], cpT[:, hd % 2, m, :],
                                                  start=(m == 0), stop=(m == 1))
                    done(mm, "co", l, hd)

                for hd in range(CH):
                    cross_scores(hd)
                    if hd:
                        cross_out(hd - 1)
                cross_out(CH - 1)
                all_taken(*[("co", l, hd) for hd in range(CH)])
                for cb in range(2):
                    rows_product([("o", l, cb, t) for t in range(TT)], yT, "o", l, cb)

                pe.wait_ge(s["hs_ready"], 4 + 3 * l)
                transposes_of_rows(l, "ffn", hs)
                xT_written(l, "ffn")
                if l == 0:
                    down = [None] * 4
                    for step in range(NJ + 2):
                        if step < NJ:
                            banks = [claim("gu", step, t) for t in range(TT)]
                            for kh in range(2):
                                w = arrived(("dense_gu", step, kh)).rearrange("p (k n) -> p k n", k=4)
                                for t in range(TT):
                                    for k in range(4):
                                        kk = 4 * kh + k
                                        mm = nc.tensor.matmul(banks[t], xT[:, kk, t * P:(t + 1) * P], w[:, k, :],
                                                              start=(kk == 0), stop=(kk == KC - 1))
                                    if kh:
                                        done(mm, "gu", step, t)
                        if step >= 2:
                            j = step - 2
                            if j == 0:
                                down = [claim("down", b) for b in range(4)]
                            w = arrived(("dense_down", j)).rearrange("p (k n) -> p k n", k=2)
                            all_taken(("hT", j, 0), ("hT", j, 1))
                            for t in range(TT):
                                for n in range(2):
                                    for k in range(2):
                                        mm = nc.tensor.matmul(down[2 * t + n], hT[:, j % 2, k, t * P:(t + 1) * P],
                                                              w[:, k, 512 * n:512 * n + 512],
                                                              start=(j == 0 and k == 0), stop=(j == NJ - 1 and k == 1),
                                                              skip_group_check=True)
                                    if j == NJ - 1:
                                        done(mm, "down", 2 * t + n)
                        if 1 <= step <= NJ:
                            j = step - 1
                            for t in range(TT):
                                wait_taken(pe, "gu", j, t)
                                bk = claim("hT", j, t)
                                for k in range(2):
                                    mm = nc.tensor.transpose(bk[:, k * P:(k + 1) * P], hh[:, j % 2, t, k * P:(k + 1) * P], ident)
                                done(mm, "hT", j, t)

            pe.wait_ge(router_in, 16)
            bk = claim("logits")
            for t in range(TT):
                for k in range(KC):
                    mm = nc.tensor.matmul(bk[:, 8 * t:8 * t + 8], xT[:, k, t * P:(t + 1) * P], wrt[:, k, :],
                                          start=(k == 0), stop=(k == KC - 1))
            done(mm, "logits")
            pe.wait_ge(s["mask_ready"], 1)
            bk = claim("rank")
            mask = rt[:, 0]
            nc.tensor.matmul(bk[:, 0:8], c("tri_lt"), mask[:, 0:8], start=True, stop=True)
            nc.tensor.matmul(bk[:, 8:16], c("tri_lt"), mask[:, 8:16], start=True, stop=False)
            nc.tensor.matmul(bk[:, 8:16], ones, mask[:, 0:8], start=False, stop=True)
            nc.tensor.matmul(bk[:, 16:24], ones, mask[:, 0:8], start=True, stop=False)
            mm = nc.tensor.matmul(bk[:, 16:24], ones, mask[:, 8:16], start=False, stop=True)
            done(mm, "rank")

            def expert_round(r):
                pe.wait_ge(s["gsel_ready"], r + 1)
                for i in range(4):
                    bk = claim("scT", r, i)
                    for x in range(4):
                        o = (4 * i + x) * P
                        mm = nc.tensor.transpose(bk[:, x * P:(x + 1) * P], gsel[:, o:o + P], ident)
                    done(mm, "scT", r, i)
                pe.wait_ge(s["sel_ready"], r + 1)
                with pe.Fori(0, NE) as e:
                    for i in range(2):
                        bk = claim("xg", r, i, e=e)
                        for x in range(4):
                            ch = 4 * i + x
                            for t in range(TT):
                                mm = nc.tensor.matmul(bk[:, x * P:(x + 1) * P], hs[:, t, ch * P:(ch + 1) * P],
                                                      sel[:, bass.ds(e * 256 + t * P, P)], start=(t == 0), stop=(t == 1))
                        done(mm, "xg", r, i)
                    for i in range(2):
                        wait_taken(pe, "xg", r, i, e=e)
                    for step in range(NJ + 2):
                        if step < NJ:
                            bk = claim("egu", r, step, e=e)
                            for kh in range(2):
                                w = arrived(("expert_gu", step, kh), e, r).rearrange("p (k n) -> p k n", k=4)
                                for k in range(4):
                                    kk = 4 * kh + k
                                    mm = nc.tensor.matmul(bk, xg[:, kk, :], w[:, k, :], start=(kk == 0), stop=(kk == KC - 1))
                            done(mm, "egu", r, step)
                        if step >= 2:
                            j = step - 2
                            if j == 0:
                                ey = [claim("ey", r, n, e=e) for n in range(2)]
                            w = arrived(("expert_down", j), e, r).rearrange("p (k n) -> p k n", k=2)
                            wait_taken(pe, "ehT", r, j, e=e)
                            for n in range(2):
                                for k in range(2):
                                    mm = nc.tensor.matmul(ey[n], hT[:, j % 2, k, 0:P], w[:, k, 512 * n:512 * n + 512],
                                                          start=(j == 0 and k == 0), stop=(j == NJ - 1 and k == 1),
                                                          skip_group_check=True)
                                if j == NJ - 1:
                                    done(mm, "ey", r, n)
                        if 1 <= step <= NJ:
                            j = step - 1
                            wait_taken(pe, "egu", r, j, e=e)
                            bk = claim("ehT", r, j, e=e)
                            for k in range(2):
                                mm = nc.tensor.transpose(bk[:, k * P:(k + 1) * P], hh[:, j % 2, 0, k * P:(k + 1) * P], ident)
                            done(mm, "ehT", r, j)
                    for n in range(2):
                        wait_taken(pe, "ey", r, n, e=e)
                    pe.wait_ge(s["sc_ready"], e + (1 + r * NE))
                    for t in range(TT):
                        for n in range(2):
                            i = 2 * t + n
                            bk = claim("eo", r, i, e=e)
                            mm = nc.tensor.matmul(bk, sc_cur[:, t * P:(t + 1) * P], ye[:, 512 * n:512 * n + 512],
                                                  start=True, stop=True)
                            done(mm, "eo", r, i)

            expert_round(0)
            for b in range(8):
                seen[b] = min(n for k, (bb_, n) in uses.items() if bb_ == b and k[0] in ("scT", "xg", "egu", "ehT", "ey", "eo") and k[1] == 1)
            pe.wait_ge(s["flag_ready"], 1)
            more = pe.value_load(flag[0:1, 0:1], min_val=0, max_val=1)
            with pe.If(more):
                expert_round(1)

        @block.scalar
        def _(act):
            ch = Chain(act, act_step)
            for l in range(DEPTH):
                for n, r in ((("ssm_lambda_re", "lam_re")), ("ssm_lambda_im", "lam_im")):
                    act.dma_start(rows_in[ROW[r, l]:ROW[r, l] + 8, :],
                                  a[n][l].rearrange("(i g) n -> i (g n)", g=2)).then_inc(rows_landed, 16)
                act.dma_start(ldt[0:2, l].rearrange("g (i o) -> g i o", o=1),
                              a["ssm_log_dt"][l].rearrange("(i g o) -> g i o", g=2, o=1), allow_slow_non_contiguous=True).then_inc(rows_landed, 16)
                for n, r in (("mix_norm_w", "mix_norm"), ("cross_norm_w", "cross_norm"), ("ffn_norm_w", "ffn_norm"),
                             ("mix_out_gain", "gain"), ("ssm_d", "ssm_d")):
                    w = a[n][l].rearrange("(r p) -> r p", p=P)
                    act.dma_start(rows_in[ROW[r, l]:ROW[r, l] + w.shape[0], :], w).then_inc(rows_landed, 16)
            act.dma_start(rows_in[ROW["mem_norm", 0]:ROW["mem_norm", 0] + 8, :],
                          a["mem_norm_w"].rearrange("(r p) -> r p", p=P)).then_inc(rows_landed, 16)
            act.dma_start(rows_in[ROWS:P, :], a["consts"][0:P - ROWS, 0:P]).then_inc(rows_landed, 16)
            def load_ssm(l):
                for r, n in enumerate(("ssm_b_re", "ssm_b_im")):
                    act.dma_start(braw[:, r], a[n][l].rearrange("(i g) n x -> (g n) i x", g=2)).then_inc(ssm_in, 16)
                for r, n in enumerate(("ssm_c_re", "ssm_c_im")):
                    w = a[n][l].rearrange("(f g) x n -> (g x) f n", f=2)
                    for dup in range(2):
                        act.dma_start(craw[:, :, r, dup, :], w).then_inc(ssm_in, 16)
                act.dma_start(wglu[:, :, :], a["ssm_w_glu"][l].rearrange("(k p) n -> p k n", p=P)).then_inc(ssm_in, 16)

            load_ssm(0)
            act.dma_start(wrt[:, :, :], a["w_router"][0].rearrange("(k p) e -> p k e", p=P)).then_inc(router_in, 16)

            norm_no = [0]

            def row_norm(src, after=None, l=None):
                n = norm_no[0]
                norm_no[0] += 1
                if after == "down":
                    for b in range(4):
                        wait_taken(act, "down", b)
                elif after:
                    for k in range(2):
                        for t in range(TT):
                            wait_taken(act, after, l, k, t)
                o = 4 * n
                for t in range(TT):
                    ch.do(nc.scalar.activation(sqj, src[:, t, :], ACT.Square, accum_out=stat[:, o + t:o + t + 1]))
                    ch.settle()
                ch.do(nc.scalar.activation(stat[:, o + 2:o + 4], stat[:, o:o + 2], ACT.Ln, bias=eps[:, 0:1], scale=1.0 / D))
                ch.settle()
                nc.scalar.activation(stat[:, o:o + 2], stat[:, o + 2:o + 4], ACT.Exp, scale=-0.5).then_inc(s["rstd_ready"], 1)

            act.wait_ge(s["eps_ready"], 1)
            act.wait_ge(mem_in, 32)
            row_norm(memT.rearrange("p (t c) s -> p t (c s)", t=TT))
            wait_taken(act, "cols")
            nc.scalar.activation(sp[:, 1, :], cols[:, P:P + DEPTH * NT], ACT.Exp).then_inc(s["sp_dt"], 1)
            act.wait_ge(x_in, 16)
            row_norm(h)
            act.wait_ge(s["sp_range"], 1)
            ch.do(nc.scalar.activation(sp[:, 4, :], sp[:, 2, :], ACT.Exp))
            ch.do(nc.scalar.activation(sp[:, 5, :], sp[:, 3, :], ACT.Sin))
            ch.do(nc.scalar.activation(sp[:, 6, :], sp[:, 3, :], ACT.Sin, scale=0.5))
            ch.settle()
            nc.scalar.copy(sp[:, 7, :], sp[:, 6, :]).then_inc(s["sp_sin"], 1)

            for l in range(DEPTH):
                if l:
                    row_norm(h, "down")
                def evacuate(key, dst, scale=None):
                    wait_filled(act, *key)
                    if scale is None:
                        free(nc.scalar.copy(dst, bank(key)), *key)
                    else:
                        free(nc.scalar.mul(dst, bank(key), scale), *key)

                def two(dst, i):
                    return dst[:, 2 * i:2 * i + 2, :].rearrange("p c s -> p (c s)")

                evacuate(("u", l), uT.rearrange("p c s -> p (c s)"))
                for i in range(NT):
                    evacuate(("bu", l, i), zone_b[:, i].rearrange("p r s -> p (r s)"))
                for name, dst, sc in (("sq", sqT, DH ** -0.5), ("sk", skT, None)):
                    for i in range(2):
                        evacuate((name, l, i), two(dst, i), sc)
                for t in range(TT):
                    wait_filled(act, "rvg", l, t)
                    ch.do(nc.scalar.copy(rvg[:, t, 0:256], bank(("rvg", l, t))[:, 0:256]))
                    ch.settle()
                    free(nc.scalar.activation(rvg[:, t, 256:512], bank(("rvg", l, t))[:, 256:512], ACT.Silu), "rvg", l, t)
                for t in range(TT):
                    evacuate(("sv", l, t), sv[:, t, :])
                for w_ in range(2):
                    evacuate(("rT", l, w_), two(rqkT, w_))
                act.wait_ge(s["rgn_sq"], l + 1)
                ch.do(nc.scalar.activation(stat[:, 40:48], stat[:, 32:40], ACT.Ln, bias=eps[:, 0:1], scale=1.0 / DH))
                ch.settle()
                nc.scalar.activation(stat[:, 48:56], stat[:, 40:48], ACT.Exp, scale=-0.5).then_inc(s["rgn_rstd"], 1)

                for step in range(SH + 1):
                    if step < SH:
                        hd = step
                        wait_filled(act, "sz", l, hd)
                        t_ = sa[:, hd % 2]
                        if hd >= 2:
                            act.wait_ge(s["slf_ready"], SH * l + hd - 1)
                        ch.do(nc.scalar.activation(t_, bank(("sz", l, hd))[:, 0:384], ACT.Abs))
                        ch.settle()
                        ch.do(nc.scalar.activation(t_, t_, ACT.Exp, scale=-1.0))
                        ch.settle()
                        nc.scalar.activation(t_, t_, ACT.Ln, bias=1.0).then_inc(s["sa_ready"], 1)
                    if step >= 1:
                        hd = step - 1
                        wait_taken(act, "sc", l, hd)
                        nc.scalar.activation(sw[:, hd % 2], sw[:, hd % 2], ACT.Exp).then_inc(s["sw_ready"], 1)
                for i in range(2):
                    evacuate(("so", l, i), two(yT, 2 + i))
                for i in range(4):
                    evacuate(("kT", l, i), two(kT, i))
                for cb in range(2):
                    for t in range(TT):
                        evacuate(("v", l, cb, t), vr[:, t, 512 * cb:512 * cb + 512])
                wait_filled(act, "y", l)
                for i in range(2):
                    wait_taken(act, "so", l, i)
                nc.scalar.activation(sq_c.rearrange("p c s -> p (c s)"), yT[:, 4:8, :].rearrange("p c s -> p (c s)"),
                                     ACT.Square).then_inc(s["sqc_ready"], 1)
                wait_taken(act, "y", l)
                nc.scalar.activation(gT.rearrange("p c s -> p (c s)"), glu_s.rearrange("p c s -> p (c s)"),
                                     ACT.Gelu_apprx_tanh).then_inc(s["gelu_ready"], 1)
                wait_filled(act, "glu", l)
                free(nc.scalar.activation(glu_s.rearrange("p c s -> p (c s)"), bank(("glu", l)), ACT.Sigmoid), "glu", l)
                if l + 1 < DEPTH:
                    load_ssm(l + 1)
                act.wait_ge(s["glu_ready"], l + 1)
                nc.scalar.activation(sq_a.rearrange("p c s -> p (c s)"), gT.rearrange("p c s -> p (c s)"),
                                     ACT.Square).then_inc(s["sqa_ready"], 1)
                for key, n, dst, sig in (("ssa", 256, rstd_a, "rstda"), ("ssc", 512, rstd_c, "rstdc")):
                    wait_filled(act, key, l)
                    free(nc.scalar.activation(dst, bank((key, l))[:, 0:256], ACT.Ln, bias=eps[:, 0:1], scale=1.0 / n), key, l)
                    wait_taken(act, key, l)
                    nc.scalar.activation(dst, dst, ACT.Exp, scale=-0.5).then_inc(s[sig], 1)

                row_norm(h, "out", l)
                for i in range(4):
                    evacuate(("q", l, i), two(cqT, i), 256 ** -0.5)
                for hd in range(CH):
                    act.wait_ge(s["cs_max"], CH * l + hd + 1)
                    if hd >= 2:
                        wait_filled(act, "cp", l, hd - 2)
                    for t in range(TT):
                        ch.do(nc.scalar.activation(cp[:, hd % 2, t, :], bank(("cs", l, hd))[:, 256 * t:256 * t + 256], ACT.Exp,
                                                   bias=stat[:, 56 + t:57 + t], accum_out=stat[:, 58 + t:59 + t]))
                    ch.settle()
                    nc.scalar.copy(stat[:, 63:64], stat[:, 61:62]).then_inc(s["cp_exp"], 1)
                    evacuate(("cp", l, hd), cpT[:, hd % 2].rearrange("p m s -> p (m s)"))

                row_norm(h, "o", l)
                if l == 0:
                    for step in range(NJ + 1):
                        if step < NJ:
                            for t in range(TT):
                                wait_filled(act, "gu", step, t)
                                nc.scalar.activation(sg[:, t], bank(("gu", step, t))[:, 0:256], ACT.Silu).then_inc(s["sg_ready"], 1)
                        if step >= 1:
                            j = step - 1
                            for t in range(TT):
                                wait_filled(act, "hT", j, t)
                                free(nc.scalar.copy(hT[:, j % 2, :, t * P:(t + 1) * P],
                                                    bank(("hT", j, t))[:, 0:256].rearrange("p (k s) -> p k s", k=2)), "hT", j, t)

            act.wait_ge(s["gate_in"], 1)
            nc.scalar.activation(rt[:, 2, 0:2], rt[:, 1, 0:2], ACT.Exp).then_inc(s["gate_exp"], 1)

            def expert_round(r):
                for i in range(4):
                    wait_filled(act, "scT", r, i)
                    free(nc.scalar.copy(scT[:, 512 * i:512 * i + 512], bank(("scT", r, i))), "scT", r, i)
                for i in range(4):
                    wait_taken(act, "scT", r, i)
                with act.Fori(0, NE) as e:
                    b, n = uses["eo", r, 3]
                    act.wait_ge(bank_filled[b], e * per_expert[b] + (n + 1 - per_expert[b]))
                    nc.scalar.copy(sc_cur, scT[:, bass.ds(e * 256, 256)]).then_inc(s["sc_ready"], 1)
                    for step in range(NJ + 1):
                        if step < NJ:
                            wait_filled(act, "egu", r, step, e=e)
                            nc.scalar.activation(sg[:, step % 2], bank(("egu", r, step))[:, 0:256], ACT.Silu).then_inc(s["sg_ready"], 1)
                        if step >= 1:
                            j = step - 1
                            wait_filled(act, "ehT", r, j, e=e)
                            free(nc.scalar.copy(hT[:, j % 2, :, 0:P],
                                                bank(("ehT", r, j))[:, 0:256].rearrange("p (k s) -> p k s", k=2)), "ehT", r, j)
                    for n_ in range(2):
                        wait_filled(act, "ey", r, n_, e=e)
                        free(nc.scalar.copy(ye[:, 512 * n_:512 * n_ + 512], bank(("ey", r, n_))), "ey", r, n_)

            expert_round(0)
            act.wait_ge(s["flag_ready"], 1)
            more = act.value_load(flag[0:1, 0:1], min_val=0, max_val=1)
            with act.If(more):
                expert_round(1)
            act.dma_start(fin_w, a["final_norm_w"].rearrange("(o d) -> o d", o=1).to_broadcast([P, D])).then_inc(finw_in, 16)
            act.wait_ge(s["h_final"], 1)
            row_norm(h)

        @block.vector
        def _(dve):
            ch = Chain(dve, dve_step)
            v = nc.vector

            def tt(out_, x, y, op):
                ch.do(v.tensor_tensor(out_, x, y, op))

            nc.vector.memset(eps[:, :], EPS).then_inc(s["eps_ready"], 1)
            ch.do(v.memset(stat[:, 60:64], 0.0))

            norm_no = [0]

            def scale_rows(src):
                n = norm_no[0]
                norm_no[0] += 1
                dve.wait_ge(s["rstd_ready"], n + 1)
                for t in range(TT):
                    ins = v.tensor_scalar(hs[:, t, :], src[:, t, :], stat[:, 4 * n + t:4 * n + t + 1], None, ALU.mult)
                    if t == TT - 1:
                        ins.then_inc(s["hs_ready"], 1)
                    else:
                        ch.do(ins)
                ch.settle()

            def scaled_transposes(l, which, dst, weight, wl):
                for i in range(4):
                    wait_filled(dve, "normT", l, which, i)
                    w = cols[:, ROW[weight, wl] + 2 * i:ROW[weight, wl] + 2 * i + 2]
                    free(v.tensor_tensor(dst[:, 2 * i:2 * i + 2, :], bank(("normT", l, which, i)).rearrange("p (c s) -> p c s", c=2),
                                         w.rearrange("p (c o) -> p c o", o=1).to_broadcast([P, 2, 256]), ALU.mult), "normT", l, which, i)

            scale_rows(memT.rearrange("p (t c) s -> p t (c s)", t=TT))
            wait_filled(dve, "cols")
            free(v.tensor_copy(cols[:, :], bank(("cols",))[:, 0:P + DEPTH * NT]), "cols")
            wait_taken(dve, "cols")
            dve.wait_ge(s["hs_ready"], 1)
            scaled_transposes("mem", 0, memT, "mem_norm", 0)
            dve.wait_ge(s["sp_dt"], 1)
            lam = cols[:, 0:32].rearrange("p (l q i) -> p l q i", l=2, q=2)

            def spv(i):
                return sp[:, i, :].rearrange("p (l i) -> p l i", l=2)

            tt(spv(2), lam[:, :, 0, :], spv(1), ALU.mult)
            tt(spv(8), lam[:, :, 1, :], spv(1), ALU.mult)
            ch.settle()
            ch.do(v.tensor_scalar(sp[:, 9, :], sp[:, 8, :], 1.0 / (2 * math.pi), None, ALU.mult))
            ch.settle()
            ch.do(v.tensor_scalar(sp[:, 10, :], sp[:, 9, :], ROUNDER, None, ALU.add))
            ch.settle()
            ch.do(v.tensor_scalar(sp[:, 9, :], sp[:, 10, :], ROUNDER, None, ALU.subtract))
            ch.settle()
            ch.do(v.scalar_tensor_tensor(out=sp[:, 10, :], in0=sp[:, 9, :], scalar=-TWO_PI_HI, in1=sp[:, 8, :], op0=ALU.mult, op1=ALU.add))
            ch.settle()
            ch.do(v.scalar_tensor_tensor(out=sp[:, 11, :], in0=sp[:, 9, :], scalar=-TWO_PI_LO, in1=sp[:, 10, :], op0=ALU.mult, op1=ALU.add))
            ch.settle()
            v.tensor_scalar(sp[:, 3, :], sp[:, 11, :], 3.1415925, -3.1415925, ALU.min, ALU.max).then_inc(s["sp_range"], 1)
            scale_rows(h)
            dve.wait_ge(s["sp_sin"], 1)
            tt(sp[:, 8, :], sp[:, 6, :], sp[:, 7, :], ALU.mult)
            ch.settle()
            ch.do(v.tensor_scalar(sp[:, 12, :], sp[:, 8, :], -2.0, 1.0, ALU.mult, ALU.add))
            ch.settle()
            tt(sp[:, 13, :], sp[:, 12, :], sp[:, 4, :], ALU.mult)
            tt(sp[:, 14, :], sp[:, 5, :], sp[:, 4, :], ALU.mult)
            tt(spv(15), lam[:, :, 0, :], lam[:, :, 0, :], ALU.mult)
            tt(spv(16), lam[:, :, 1, :], lam[:, :, 1, :], ALU.mult)
            ch.settle()
            tt(sp[:, 17, :], sp[:, 15, :], sp[:, 16, :], ALU.add)
            ch.do(v.tensor_scalar(sp[:, 13, :], sp[:, 13, :], -1.0, None, ALU.add))
            ch.settle()
            ch.do(v.reciprocal(sp[:, 18, :], sp[:, 17, :]))
            tt(spv(15), spv(13), lam[:, :, 0, :], ALU.mult)
            tt(spv(16), spv(14), lam[:, :, 1, :], ALU.mult)
            tt(spv(17), spv(14), lam[:, :, 0, :], ALU.mult)
            tt(spv(19), spv(13), lam[:, :, 1, :], ALU.mult)
            ch.settle()
            tt(sp[:, 15, :], sp[:, 15, :], sp[:, 16, :], ALU.add)
            tt(sp[:, 17, :], sp[:, 17, :], sp[:, 19, :], ALU.subtract)
            ch.settle()
            tt(sp[:, 8, :], sp[:, 15, :], sp[:, 18, :], ALU.mult)
            v.tensor_tensor(sp[:, 9, :], sp[:, 17, :], sp[:, 18, :], ALU.mult).then_inc(s["sp_ready"], 1)
            ch.settle()
            dve.wait_ge(consts_in, 16)

            def add_to_h(keys):
                for key, t, n in keys:
                    wait_filled(dve, *key)
                    hv = h[:, t, 512 * n:512 * n + 512]
                    free(v.tensor_tensor(hv, hv, bank(key), ALU.add), *key)
                for key, t, n in keys:
                    wait_taken(dve, *key)

            for l in range(DEPTH):
                if l:
                    scale_rows(h)
                scaled_transposes(l, "mix", xT, "mix_norm", l)
                cos = c("rope_cos").rearrange("p (t q o f) -> p t q o f", t=2, q=2, o=1)
                sin = c("rope_sin").rearrange("p (t q o f) -> p t q o f", t=2, q=2, o=1)
                for t in range(TT):
                    wait_filled(dve, "rqk", l, t)
                    src = bank(("rqk", l, t)).rearrange("p (q h x f) -> p q h x f", q=2, h=RH, x=2)
                    dst = rqk[:, t, :].rearrange("p (q h x f) -> p q h x f", q=2, h=RH, x=2)
                    t1 = rtmp[:, 0].rearrange("p (q h f) -> p q h f", q=2, h=RH)
                    t2 = rtmp[:, 1].rearrange("p (q h f) -> p q h f", q=2, h=RH)
                    cb_ = cos[:, t].to_broadcast([P, 2, RH, 32])
                    sb_ = sin[:, t].to_broadcast([P, 2, RH, 32])
                    tt(t1, src[:, :, :, 0, :], cb_, ALU.mult)
                    tt(t2, src[:, :, :, 1, :], sb_, ALU.mult)
                    ch.settle()
                    tt(dst[:, :, :, 0, :], t1, t2, ALU.subtract)
                    ch.settle()
                    tt(t1, src[:, :, :, 0, :], sb_, ALU.mult)
                    free(v.tensor_tensor(t2, src[:, :, :, 1, :], cb_, ALU.mult), "rqk", l, t)
                    ch.settle()
                    wait_taken(dve, "rqk", l, t)
                    ins = v.tensor_tensor(dst[:, :, :, 1, :], t1, t2, ALU.add)
                    if t == TT - 1:
                        ins.then_inc(s["rqk_ready"], 1)
                    else:
                        ch.do(ins)
                        ch.settle()
                wait_filled(dve, "BT", l)
                free(v.tensor_copy(BT.rearrange("p f r s -> p (f r s)"), bank(("BT", l))), "BT", l)
                wait_filled(dve, "CT", l)
                cb4 = bank(("CT", l)).rearrange("p (f r s) -> p f r s", f=2, r=2)
                gm = c("group_mask").rearrange("p (o s) -> p o s", o=1).to_broadcast([P, 2, P])
                ch.do(v.tensor_tensor(CT[:, :, 0, :], cb4[:, :, 0, :], gm, ALU.mult))
                ch.settle()
                free(v.scalar_tensor_tensor(out=CT[:, :, 1, :], in0=cb4[:, :, 1, :], scalar=-1.0, in1=gm, op0=ALU.mult, op1=ALU.mult), "CT", l)

                dve.wait_ge(s["rot_ready"], l + 1)
                for g in range(4):
                    wait_taken(dve, "bu", l, 2 * g)
                    wait_taken(dve, "bu", l, 2 * g + 1)
                    if l or g:
                        dve.wait_ge(s["x_im"], 4 * l + g)
                    pre, pim = rot_tab[:, 0, 2 * g:2 * g + 2, :], rot_tab[:, 1, 2 * g:2 * g + 2, :]
                    bre, bim = zone_b[:, 2 * g:2 * g + 2, 0, :], zone_b[:, 2 * g:2 * g + 2, 1, :]
                    tt(yin[:, 0], pre, bre, ALU.mult)
                    tt(vtmp, pim, bim, ALU.mult)
                    ch.settle()
                    tt(yin[:, 0], yin[:, 0], vtmp, ALU.add)
                    ch.settle()
                    for r in range(2):
                        if r == 1:
                            dve.wait_ge(s["yin_im"], 4 * l + g + 1)
                        for i in range(2):
                            mag = sp[:, 4, 8 * l + 2 * g + i:8 * l + 2 * g + i + 1]
                            ins = v.tensor_tensor_scan(ysc[:, r, i, :], mag.to_broadcast([P, S]), yin[:, r, i, :], 0.0, ALU.mult, ALU.add)
                            if r and i:
                                ins.then_inc(s["ysc_ready"], 1)
                            else:
                                ch.do(ins)
                    ch.settle()
                    dve.wait_ge(s["ysc_ready"], 4 * l + g + 1)
                    tt(bre, pre, ysc[:, 0], ALU.mult)
                    tt(vtmp, pim, ysc[:, 1], ALU.mult)
                    ch.settle()
                    v.tensor_tensor(bre, bre, vtmp, ALU.subtract).then_inc(s["x_re"], 1)
                dve.wait_ge(s["x_re"], 4 * l + 4)

                dec = c("decay").rearrange("p (h s) -> p h s", h=RH)
                for hd in range(RH):
                    wait_filled(dve, "rs", l, hd)
                    bk = bank(("rs", l, hd))
                    ch.do(v.tensor_tensor(rsc[:, hd % 2, 0:256], bk[:, 0:256], dec[:, hd, :], ALU.mult))
                    ch.settle()
                    free(v.tensor_tensor(rsc[:, hd % 2, 256:384], bk[:, 256:384], dec[:, hd, 0:P], ALU.mult), "rs", l, hd)
                wait_filled(dve, "ro", l)
                ob = bank(("ro", l)).rearrange("p (g f) -> p g f", g=8)
                rog = ro.rearrange("p t (h f) -> p (t h) f", h=RH)
                ro2g = ro2.rearrange("p t (h f) -> p (t h) f", h=RH)
                mu, dev = stat[:, 32:40], stat[:, 48:56]

                def wide(x):
                    return x.rearrange("p (g o) -> p g o", o=1).to_broadcast([P, 8, DH])

                ch.do(v.tensor_reduce(mu, ob, AX_X, ALU.add))
                ch.settle()
                ch.do(v.tensor_scalar(mu, mu, 1.0 / DH, None, ALU.mult))
                ch.settle()
                free(v.tensor_tensor(rog, ob, wide(mu), ALU.subtract), "ro", l)
                wait_taken(dve, "ro", l)
                tt(ro2g, rog, rog, ALU.mult)
                ch.settle()
                v.tensor_reduce(mu, ro2g, AX_X, ALU.add).then_inc(s["rgn_sq"], 1)
                dve.wait_ge(s["rgn_rstd"], l + 1)
                tt(rog, rog, wide(dev), ALU.mult)
                ch.settle()
                v.tensor_tensor(ro, ro, rvg[:, :, 256:512], ALU.mult).then_inc(s["yb_ready"], 1)

                for step in range(SH + 1):
                    if step < SH:
                        hd = step
                        dve.wait_ge(s["sa_ready"], SH * l + hd + 1)
                        lf = slf[:, hd % 2]
                        free(v.scalar_tensor_tensor(out=lf, in0=bank(("sz", l, hd))[:, 0:384], scalar=0.0, in1=sa[:, hd % 2],
                                                    op0=ALU.max, op1=ALU.add), "sz", l, hd)
                        wait_taken(dve, "sz", l, hd)
                        v.tensor_tensor(lf, lf, c("neg_mask"), ALU.mult).then_inc(s["slf_ready"], 1)
                    if step >= 1:
                        hd = step - 1
                        wait_filled(dve, "sc", l, hd)
                        free(v.scalar_tensor_tensor(out=sw[:, hd % 2], in0=bank(("sc", l, hd))[:, 0:384], scalar=0.0,
                                                    in1=c("mask_bias"), op0=ALU.min, op1=ALU.add), "sc", l, hd)

                wait_filled(dve, "ybT", l)
                g2 = cols[:, ROW["gain", l] + 2:ROW["gain", l] + 4]
                free(v.tensor_tensor(yT[:, 2:4, :], bank(("ybT", l)).rearrange("p (c s) -> p c s", c=2),
                                     g2.rearrange("p (c o) -> p c o", o=1).to_broadcast([P, 2, 256]), ALU.mult), "ybT", l)
                wait_filled(dve, "y", l)
                for cc in range(2):
                    ins = v.scalar_tensor_tensor(out=glu_s[:, cc, :], in0=uT[:, cc, :], scalar=col("ssm_d", l, cc),
                                                 in1=bank(("y", l))[:, 256 * cc:256 * cc + 256], op0=ALU.mult, op1=ALU.add)
                    if cc:
                        free(ins, "y", l)
                    else:
                        ch.do(ins)
                        ch.settle()
                wait_taken(dve, "glu", l)
                v.tensor_tensor(gT, gT, glu_s, ALU.mult).then_inc(s["glu_ready"], 1)
                dve.wait_ge(s["glu_ready"], l + 1)
                dve.wait_ge(s["rstda"], l + 1)
                for cc in range(2):
                    ins = v.scalar_tensor_tensor(out=yT[:, cc, :], in0=gT[:, cc, :], scalar=col("gain", l, cc), in1=rstd_a,
                                                 op0=ALU.mult, op1=ALU.mult)
                    ch.do(ins)
                ch.settle()
                v.tensor_copy(stat[:, 60:61], stat[:, 62:63]).then_inc(s["ya_T"], 1)
                dve.wait_ge(s["rstdc"], l + 1)
                for cc in range(4):
                    ch.do(v.scalar_tensor_tensor(out=yT[:, 4 + cc, :], in0=yT[:, 4 + cc, :], scalar=col("gain", l, 4 + cc), in1=rstd_c,
                                                 op0=ALU.mult, op1=ALU.mult))
                ch.settle()
                v.tensor_copy(stat[:, 60:61], stat[:, 62:63]).then_inc(s["yc_T"], 1)
                add_to_h([(("out", l, n, t), t, n) for n in range(2) for t in range(TT)])

                scale_rows(h)
                scaled_transposes(l, "cross", xT, "cross_norm", l)

                def head_out(hd):
                    wait_filled(dve, "co", l, hd)
                    free(v.tensor_copy(yT[:, 2 * hd:2 * hd + 2, :].rearrange("p c s -> p (c s)"), bank(("co", l, hd))), "co", l, hd)

                for hd in range(CH):
                    wait_filled(dve, "cs", l, hd)
                    ch.do(v.tensor_reduce(cstat[:, 0:2], bank(("cs", l, hd)).rearrange("p (t s) -> p t s", t=2), AX_X, ALU.max))
                    ch.settle()
                    v.tensor_scalar(stat[:, 56:58], cstat[:, 0:2], -1.0, None, ALU.mult).then_inc(s["cs_max"], 1)
                    dve.wait_ge(s["cp_exp"], CH * l + hd + 1)
                    free(v.reciprocal(cstat[:, 2:4], stat[:, 58:60]), "cs", l, hd)
                    wait_taken(dve, "cs", l, hd)
                    for t in range(TT):
                        ins = v.tensor_scalar(cp[:, hd % 2, t, :], cp[:, hd % 2, t, :], cstat[:, 2 + t:3 + t], None, ALU.mult)
                        if t:
                            ins.then_inc(s["cp_ready"], 1)
                        else:
                            ch.do(ins)
                            ch.settle()
                    if hd:
                        head_out(hd - 1)
                head_out(CH - 1)
                add_to_h([(("o", l, n, t), t, n) for n in range(2) for t in range(TT)])

                scale_rows(h)
                scaled_transposes(l, "ffn", xT, "ffn_norm", l)
                if l == 0:
                    for j in range(NJ):
                        for t in range(TT):
                            dve.wait_ge(s["sg_ready"], 2 * j + t + 1)
                            if j >= 2:
                                wait_filled(dve, "hT", j - 2, t)
                            free(v.tensor_tensor(hh[:, j % 2, t, :], sg[:, t], bank(("gu", j, t))[:, 256:512], ALU.mult), "gu", j, t)
                    add_to_h([(("down", 2 * t + n), t, n) for t in range(TT) for n in range(2)])

            def r3(i):
                return rt[:, i, :].rearrange("p (t e) -> p t e", t=2)

            def over_e(x):
                return x.rearrange("p (t o) -> p t o", o=1).to_broadcast([P, 2, NE])

            MASK, DIFF, EXPD, LOG, EQ, KEY, OH1, OH2, GATE, SLOTN, MX, CNT = range(12)
            key8 = c("first_key").rearrange("p (o e) -> p o e", o=1).to_broadcast([P, 2, NE])
            wait_filled(dve, "logits")
            free(v.tensor_copy(rt[:, LOG, :], bank(("logits",))[:, 0:16]), "logits")
            wait_taken(dve, "logits")
            for k, oh in enumerate((OH1, OH2)):
                m = rt[:, MX, 4 * k:4 * k + 2]
                ch.do(v.tensor_reduce(m, r3(LOG), AX_X, ALU.max))
                ch.settle()
                tt(r3(EQ), r3(LOG), over_e(m), ALU.is_equal)
                ch.settle()
                tt(r3(KEY), r3(EQ), key8, ALU.mult)
                ch.settle()
                ch.do(v.tensor_reduce(rt[:, MX, 4 * k + 2:4 * k + 4], r3(KEY), AX_X, ALU.max))
                ch.settle()
                tt(r3(oh), r3(KEY), over_e(rt[:, MX, 4 * k + 2:4 * k + 4]), ALU.is_equal)
                ch.settle()
                if k == 0:
                    ch.do(v.scalar_tensor_tensor(out=rt[:, LOG, :], in0=rt[:, OH1, :], scalar=-1e30, in1=rt[:, LOG, :],
                                                 op0=ALU.mult, op1=ALU.add))
                    ch.settle()
            v.tensor_tensor(rt[:, MASK, :], rt[:, OH1, :], rt[:, OH2, :], ALU.add).then_inc(s["mask_ready"], 1)
            v.tensor_tensor(rt[:, DIFF, 0:2], rt[:, MX, 4:6], rt[:, MX, 0:2], ALU.subtract).then_inc(s["gate_in"], 1)
            dve.wait_ge(s["gate_exp"], 1)
            ch.do(v.tensor_scalar(rt[:, EXPD, 2:4], rt[:, EXPD, 0:2], 1.0, None, ALU.add))
            ch.settle()
            ch.do(v.reciprocal(rt[:, EXPD, 4:6], rt[:, EXPD, 2:4]))
            ch.settle()
            tt(rt[:, EXPD, 6:8], rt[:, EXPD, 4:6], rt[:, EXPD, 0:2], ALU.mult)
            tt(r3(OH1), r3(OH1), over_e(rt[:, EXPD, 4:6]), ALU.mult)
            ch.settle()
            tt(r3(OH2), r3(OH2), over_e(rt[:, EXPD, 6:8]), ALU.mult)
            ch.settle()
            tt(rt[:, GATE, :], rt[:, OH1, :], rt[:, OH2, :], ALU.add)
            ch.settle()
            wait_filled(dve, "rank")
            rk = bank(("rank",))
            ch.do(v.tensor_reduce(rt[:, CNT, 0:1], rk[:, 16:24], AX_X, ALU.max))
            free(v.scalar_tensor_tensor(out=rt[:, SLOTN, :], in0=rk[:, 0:16], scalar=1.0, in1=rt[:, MASK, :], op0=ALU.add, op1=ALU.mult), "rank")
            ch.settle()
            wait_taken(dve, "rank")
            v.tensor_scalar(flag[:, :], rt[:, CNT, 0:1], float(ROUND) + 0.5, None, ALU.is_ge).then_inc(s["flag_ready"], 1)

            def expert_round(r):
                if r:
                    wait_filled(dve, "eo", 0, 3, e=NE - 1)
                ch.do(v.tensor_scalar(rt[:, EQ, :], rt[:, SLOTN, :], -1.0 - r * ROUND, None, ALU.add))
                ch.settle()

                def spread(x):
                    return x.rearrange("p (t e o) -> p e t o", t=2, o=1).to_broadcast([P, NE, 2, P])

                io = c("iota").rearrange("p (a b s) -> p a b s", a=1, b=1).to_broadcast([P, NE, 2, P])
                sel4 = sel.rearrange("p (e t s) -> p e t s", e=NE, t=2)
                gsel4 = gsel.rearrange("p (e t s) -> p e t s", e=NE, t=2)
                v.tensor_tensor(sel4, spread(rt[:, EQ, :]), io, ALU.is_equal).then_inc(s["sel_ready"], 1)
                dve.wait_ge(s["sel_ready"], r + 1)
                v.tensor_tensor(gsel4, sel4, spread(rt[:, GATE, :]), ALU.mult).then_inc(s["gsel_ready"], 1)
                fw = cols[:, ROW["ffn_norm", 1]:ROW["ffn_norm", 1] + 8].rearrange("p (c o) -> p c o", o=1)
                with dve.Fori(0, NE) as e:
                    for i in range(2):
                        wait_filled(dve, "xg", r, i, e=e)
                        free(v.tensor_tensor(xg[:, 4 * i:4 * i + 4, :], bank(("xg", r, i)).rearrange("p (c s) -> p c s", c=4),
                                             fw[:, 4 * i:4 * i + 4].to_broadcast([P, 4, P]), ALU.mult), "xg", r, i)
                    for j in range(NJ):
                        dve.wait_ge(s["sg_ready"], e * NJ + (2 * NJ + j + 1 + r * NE * NJ))
                        if j >= 2:
                            wait_filled(dve, "ehT", r, j - 2, e=e)
                        free(v.tensor_tensor(hh[:, j % 2, 0, :], sg[:, j % 2], bank(("egu", r, j))[:, 256:512], ALU.mult), "egu", r, j)
                    for t in range(TT):
                        for n_ in range(2):
                            i = 2 * t + n_
                            wait_filled(dve, "eo", r, i, e=e)
                            hv = h[:, t, 512 * n_:512 * n_ + 512]
                            free(v.tensor_tensor(hv, hv, bank(("eo", r, i)), ALU.add), "eo", r, i)

            expert_round(0)
            dve.wait_ge(s["flag_ready"], 1)
            more = dve.value_load(flag[0:1, 0:1], min_val=0, max_val=1)
            with dve.If(more):
                expert_round(1)
            v.tensor_copy(stat[:, 60:61], stat[:, 62:63]).then_inc(s["h_final"], 1)
            n = norm_no[0]
            dve.wait_ge(s["rstd_ready"], n + 1)
            dve.wait_ge(finw_in, 16)
            for t in range(TT):
                v.scalar_tensor_tensor(out=hs[:, t, :], in0=h[:, t, :], scalar=stat[:, 4 * n + t:4 * n + t + 1], in1=fin_w,
                                       op0=ALU.mult, op1=ALU.mult).then_inc(s["final_ready"], 1)

        @block.gpsimd
        def _(pool):
            ch = Chain(pool, pool_step)
            g_ = nc.gpsimd

            def tt(out_, x, y, op):
                ch.do(g_.tensor_tensor(out_, x, y, op))

            
            pool.wait_ge(s["sp_ready"], 1)
            for l in range(DEPTH):
                pool.wait_ge(ssm_in, 16 * N_SSM_LOADS * (l + 1))
                if l:
                    wait_filled(pool, "gu", 0, 0)
                ch.do(g_.memset(bb[:, :, :, :], 0.0))
                ch.settle()
                for q in range(2):
                    p0 = 64 * q
                    rows = slice(p0, p0 + 64)

                    def z(i):
                        return sp[rows, i, 8 * l:8 * l + 8].rearrange("p (i o) -> p i o", o=1).to_broadcast([64, NT, 16])

                    br, bi = braw[rows, 0], braw[rows, 1]
                    for r, (x, y, op) in enumerate(((br, bi, ALU.subtract), (bi, br, ALU.add))):
                        tt(bbt[rows, 0], z(8), x, ALU.mult)
                        tt(bbt[rows, 1], z(9), y, ALU.mult)
                        ch.settle()
                        ins = g_.tensor_tensor(bb[rows, r, :, 16 * q:16 * q + 16], bbt[rows, 0], bbt[rows, 1], op)
                        if q and r:
                            ins.then_inc(s["bb_ready"], 1)
                        else:
                            ch.do(ins)
                            ch.settle()
                pool.wait_ge(s["bb_ready"], l + 1)
                re, im = rot_tab[:, 0], rot_tab[:, 1]
                ch.do(g_.memset(re[:, :, 0:1], 1.0))
                ch.do(g_.memset(im[:, :, 0:1], 0.0))
                ch.do(g_.tensor_copy(re[:, :, 1:2], sp[:, 12, 8 * l:8 * l + 8].rearrange("p (i o) -> p i o", o=1)))
                ch.do(g_.tensor_copy(im[:, :, 1:2], sp[:, 5, 8 * l:8 * l + 8].rearrange("p (i o) -> p i o", o=1)))
                ch.settle()
                m = 1
                while m < S:
                    n = min(m, S - 1 - m)
                    if n <= 0:
                        break
                    w_ = [P, NT, n]
                    lo, hi, top = slice(1, n + 1), slice(m + 1, m + n + 1), slice(m, m + 1)
                    t1 = rot_tmp[:, 0, :, 0:n]
                    t2 = rot_tmp[:, 1, :, 0:n]
                    mr, mi = re[:, :, top].to_broadcast(w_), im[:, :, top].to_broadcast(w_)
                    tt(t1, re[:, :, lo], mr, ALU.mult)
                    tt(t2, im[:, :, lo], mi, ALU.mult)
                    ch.settle()
                    tt(re[:, :, hi], t1, t2, ALU.subtract)
                    ch.settle()
                    tt(t1, re[:, :, lo], mi, ALU.mult)
                    tt(t2, im[:, :, lo], mr, ALU.mult)
                    ch.settle()
                    tt(im[:, :, hi], t1, t2, ALU.add)
                    ch.settle()
                    m *= 2
                g_.memset(ptmp[:, 0, 0:1], 0.0).then_inc(s["rot_ready"], 1)
                pool.wait_ge(s["rot_ready"], l + 1)
                for g in range(4):
                    wait_taken(pool, "bu", l, 2 * g)
                    wait_taken(pool, "bu", l, 2 * g + 1)
                    pre, pim = rot_tab[:, 0, 2 * g:2 * g + 2, :], rot_tab[:, 1, 2 * g:2 * g + 2, :]
                    bre, bim = zone_b[:, 2 * g:2 * g + 2, 0, :], zone_b[:, 2 * g:2 * g + 2, 1, :]
                    if g:
                        pool.wait_ge(s["x_im"], 4 * l + g)
                    if l or g:
                        pool.wait_ge(s["ysc_ready"], 4 * l + g)
                    tt(yin[:, 1], pre, bim, ALU.mult)
                    tt(ptmp[:, :, :], pim, bre, ALU.mult)
                    ch.settle()
                    g_.tensor_tensor(yin[:, 1], yin[:, 1], ptmp[:, :, :], ALU.subtract).then_inc(s["yin_im"], 1)
                    pool.wait_ge(s["yin_im"], 4 * l + g + 1)
                    pool.wait_ge(s["ysc_ready"], 4 * l + g + 1)
                    tt(bim, pre, ysc[:, 1], ALU.mult)
                    tt(ptmp[:, :, :], pim, ysc[:, 0], ALU.mult)
                    ch.settle()
                    g_.tensor_tensor(bim, bim, ptmp[:, :, :], ALU.add).then_inc(s["x_im"], 1)

_INS = ["x", "mem", "mix_norm_w", "w_in", "ssm_lambda_re", "ssm_lambda_im", "ssm_b_re", "ssm_b_im", "ssm_c_re", "ssm_c_im",
        "ssm_d", "ssm_log_dt", "ssm_w_glu", "mix_out_gain", "w_out", "cross_norm_w", "mem_norm_w", "w_cross_q", "w_cross_kv",
        "w_cross_o", "ffn_norm_w", "w_dense_gu", "w_dense_down", "w_router", "w_expert_gu", "w_expert_down", "final_norm_w"]


def kernel(**inputs):
    import concourse.bacc as _bacc
    from concourse.bass_utils import run_bass_kernel_spmd as _run

    nc = _bacc.Bacc("TRN2", target_bir_lowering=False, num_devices=1, dynamic_dma_scratch_size=1024)
    arrays, args = {}, {}
    host = {n: np.ascontiguousarray(inputs[n]) for n in _INS}
    host["consts"] = constants()
    for name, v in host.items():
        arrays[f"in_{name}"] = v
        args[name] = nc.dram_tensor(f"in_{name}", v.shape, mybir.dt.from_np(v.dtype), kind="ExternalInput").ap()
    out = nc.dram_tensor("out_0", (1, S, D), F32, kind="ExternalOutput").ap()
    trunk(nc, args, out)
    r = _run(nc, [arrays], core_ids=[0])
    return r.results[0]["out_0"]
```

```python
import math
from contextlib import ExitStack

import numpy as np

import concourse.bass as bass
from concourse import mybir

F32 = mybir.dt.float32
F32R = mybir.dt.float32r
I32 = mybir.dt.int32
ACT = mybir.ActivationFunctionType
ALU = mybir.AluOpType
AX_X = mybir.AxisListType.X

P = 128
D = 1024
S = 256
DEPTH = 2
KC = D // P
TT = S // P
EPS = 1e-6
SSM_W = 256
NT = 8
RH = 4
SH = 8
DH = 64
CH = 4
F = 2816
NJ = F // 256
NE = 8
SLOTS = 11
JOBS_E = 6 * NJ
SLOT = 1024
STAGES = 6
FILLERS = (1, 3, 5)
HI_AHEAD, LO_AHEAD = 4, 1
LAG = 4
ROUND = 128
MASKED = -30000.0
TWO_PI_HI = 6.28125
TWO_PI_LO = 2 * math.pi - 6.28125
ROUNDER = 12582912.0

CONST = {}
_at = 0
for _name, _w in (("ident", 128), ("tri_ge", 128), ("ones", 128), ("tri_lt", 128), ("iota", 128),
                  ("group_mask", 128), ("neg_mask", 384), ("mask_bias", 384), ("decay", RH * 256),
                  ("rope_cos", 128), ("rope_sin", 128), ("first_key", 8), ("half", 128)):
    CONST[_name] = (_at, _at + _w)
    _at += _w
CONST_W = _at

ROW = {}
_at = 0
for _l in range(DEPTH):
    for _name, _w in (("lam_re", 8), ("lam_im", 8)):
        ROW[_name, _l] = _at
        _at += _w
for _name, _w in (("mix_norm", 8), ("cross_norm", 8), ("ffn_norm", 8), ("gain", 8), ("ssm_d", 2)):
    for _l in range(DEPTH):
        ROW[_name, _l] = _at
        _at += _w
ROW["mem_norm", 0] = _at
_at += 8
ROWS = _at


def constants():
    c = np.zeros((P, CONST_W), np.float32)

    def put(name, a):
        c[:, CONST[name][0]:CONST[name][1]] = a.reshape(P, -1)

    p = np.arange(P)
    put("ident", np.eye(P))
    put("tri_ge", (p[:, None] >= p[None, :]) * 1.0)
    put("ones", np.ones((P, P)))
    put("tri_lt", (p[:, None] < p[None, :]) * 1.0)
    put("iota", np.tile(p, (P, 1)))
    put("group_mask", ((p[None, :] // 16) % 2 == (p[:, None] >= 64)) * 1.0)
    q = np.concatenate([np.arange(256), np.arange(128)])
    strict = p[:, None] < q[None, :]
    put("neg_mask", -1.0 * strict)
    put("mask_bias", np.where(strict, 0.0, MASKED))
    lg = np.log1p(-(2.0 ** (-5.0 - np.arange(RH, dtype=np.float64))))
    rel = np.arange(256)[None, :] - p[:, None]
    put("decay", np.where(rel[:, None] >= 0, np.exp(lg[None, :, None] * np.maximum(rel, 0)[:, None]), 0.0))
    inv = (10000.0 ** (-np.arange(32, dtype=np.float32) / np.float32(32))).astype(np.float32)
    ang = (np.arange(S, dtype=np.float32)[:, None] * inv[None, :]).astype(np.float32).reshape(TT, P, 32)
    ang = ang.transpose(1, 0, 2).astype(np.float64)
    scale = np.array([1.0, DH ** -0.5])[None, None, :, None]
    put("rope_cos", np.cos(ang)[:, :, None] * scale)
    put("rope_sin", np.sin(ang)[:, :, None] * scale)
    put("first_key", np.tile(8.0 - np.arange(8), (P, 1)))
    put("half", (p[:, None] == p[None, :] // 64) * 1.0)
    return c


def plan_jobs():
    jobs = []

    def full(name, l, cb):
        jobs.extend([(name, l, cb, kq) for kq in range(4)])

    def swiglu(name):
        out = []
        for step in range(NJ + 2):
            if step < NJ:
                out += [(name + "_gu", step, kq) for kq in range(4)]
            if step >= 2:
                out += [(name + "_down", step - 2, k) for k in range(2)]
        return out

    for l in range(DEPTH):
        jobs.extend([("in_u", l, 0, kh) for kh in range(2)])
        for cb in ("rqk", "sq", "sk", "rvg", "sv"):
            full("in", l, cb)
        for name, cbs in (("kv", (0, 1, 2)), ("out", (0, 1)), ("kv", (3,)), ("q", (0, 1)), ("o", (0, 1))):
            for cb in cbs:
                full(name, l, cb)
        if l == 0:
            jobs += swiglu("dense")
    return jobs, swiglu("expert")


def plan_banks():
    uses, count = {}, [0] * 8

    def use(bank, *key):
        uses[key] = (bank, count[bank])
        count[bank] += 1

    turn = [0]

    def rot(*key, among=range(8)):
        use(among[turn[0] % len(among)], *key)
        turn[0] += 1

    rot("cols")
    for l in range(DEPTH):
        for i in range(4):
            rot("normT", l, "mix", i)
        rot("u", l)
        rot("rqk", l, 0)
        rot("rqk", l, 1)
        if l == 0:
            for i in range(4):
                rot("normT", "mem", 0, i)
        rot("BT", l)
        rot("CT", l)
        if l == 0:
            turn[0] += 2
        rot("sq", l, 0)
        rot("sq", l, 1)
        for i in range(NT):
            rot("bu", l, i)
        rot("sk", l, 0)
        rot("sk", l, 1)
        for name in ("rvg", "sv"):
            rot(name, l, 0)
            rot(name, l, 1)
        rot("rT", l, 0)
        rot("rT", l, 1)
        use(7, "ro", l)
        for h in range(RH):
            use(h % 2, "rs", l, h)
        use(2, "ybT", l)
        for h in range(SH + 2):
            if h < SH:
                use(3 + h % 3, "sz", l, h)
            if h in FILLERS:
                use(FILLERS.index(h) % 2, "kT", l, FILLERS.index(h))
            if 1 <= h <= SH:
                use(3 + (h - 1) % 3, "sc", l, h - 1)
            if h >= 2 and h % 4 == 2 and (h - 2) // 4 < 2:
                use(6 + (h - 2) // 4, "so", l, (h - 2) // 4)
        turn[0] = 0
        rot("y", l)
        rot("kT", l, 3)
        rot("glu", l)
        rot("v", l, 0, 0)
        rot("ssa", l)
        rot("ssc", l)
        rot("v", l, 0, 1)
        for n in range(2):
            rot("out", l, n, 0)
            rot("out", l, n, 1)
        rot("v", l, 1, 0)
        rot("v", l, 1, 1)
        for i in range(4):
            rot("normT", l, "cross", i)
        for i in range(4):
            rot("q", l, i)
        for h in range(CH):
            rot("cs", l, h)
            if h:
                rot("cp", l, h - 1)
                rot("co", l, h - 1)
        rot("cp", l, CH - 1)
        rot("co", l, CH - 1)
        for n in range(2):
            rot("o", l, n, 0)
            rot("o", l, n, 1)
        for i in range(4):
            rot("normT", l, "ffn", i)
        if l == 0:
            for s in range(NJ + 2):
                if s < NJ:
                    use(0 if s == 1 else 4, "gu", s, 0)
                    use(1 if s == 1 else 5, "gu", s, 1)
                if 1 <= s <= NJ:
                    use(6, "hT", s - 1, 0)
                    use(7, "hT", s - 1, 1)
            for b in range(4):
                use(b, "down", b)
        else:
            rot("logits")
            rot("rank")
            for i in range(4):
                use((0, 1, 4, 5)[i], "scT", 0, i)
    before = list(count)

    def expert(r):
        use(6, "xg", r, 0)
        use(7, "xg", r, 1)
        for step in range(NJ):
            use(2 + step % 2, "egu", r, step)
            use(4 + step % 2, "ehT", r, step)
        for n in range(2):
            use(n, "ey", r, n)
        for i in range(4):
            use((0, 1, 4, 5)[i], "eo", r, i)

    expert(0)
    per_expert = [count[b] - before[b] for b in range(8)]
    for b in range(8):
        count[b] = before[b] + NE * per_expert[b]
    for i in range(4):
        use((0, 1, 4, 5)[i], "scT", 1, i)
    expert(1)
    return uses, per_expert


def swiglu_order(engine):
    _, blocks = plan_jobs()
    no = {k[0][7:] + str(k[1:]): n for n, k in enumerate(blocks)}
    items = [(float(i), "block", i) for i in range(JOBS_E)]
    for j in range(NJ):
        gu = no["gu" + str((j, 3))] + LAG
        turn = no["down" + str((j - 1, 1))] if 1 <= j < NJ - 1 else \
            no["gu" + str((1, 3))] if j == 0 else no["down" + str((NJ - 3, 1))]
        turned = turn + LAG
        if engine == "scalar":
            items.append((gu - 0.5, "silu", j))
            items.append((turned - (1.3 if j == NJ - 2 else 0.4), "hidden", j))
        else:
            items.append((gu + 0.5, "gated", j))
            items.append((turned - 0.6 if j == NJ - 2 else turned + 0.5, "hidden", j))
    return items


def expert_order(engine):
    items = swiglu_order(engine)
    if engine == "scalar":
        items += [(20.5, "scatter_matrix", 0), (-0.6, "gathered", 0)]
        items += [(JOBS_E + LAG - 1.5, "result", 0), (JOBS_E + LAG - 1.4, "result", 1)]
    else:
        items += [(-1.4, "tokens", 0), (-0.5, "tokens_rest", 0)]
        items += [(JOBS_E + LAG + 2.6 + 0.1 * (i % 2) + i // 2, "scattered", i) for i in range(4)]
    return items


SCALAR_DENSE, VECTOR_DENSE = swiglu_order("scalar"), swiglu_order("vector")
SCALAR_EXPERT, VECTOR_EXPERT = expert_order("scalar"), expert_order("vector")


def schedule(items):
    return sorted(items, key=lambda x: x[0])


N_ROW_LOADS = 3 * DEPTH + 5 + 2
N_SSM_LOADS = 7
IN_COLS = {"u": 0, "rqk": 256, "rvg": 768, "sq": 1280, "sk": 1792, "sv": 2304}


def trunk(nc, a, out):
    jobs, expert_jobs = plan_jobs()
    job_no = {k: n for n, k in enumerate(jobs)}
    ejob_no = {k: n for n, k in enumerate(expert_jobs)}
    BASE = len(jobs)
    uses, per_expert = plan_banks()

    with ExitStack() as ctx:
        def sb(name, *shape, dt=F32):
            return ctx.enter_context(nc.sbuf_tensor(name, [P, *shape], dt))

        def sem(name):
            return ctx.enter_context(nc.semaphore(name))

        ps = ctx.enter_context(nc.psum_tensor("ps", [P, 8, 512], F32))
        def place():
            return -(-nc.sbuf_base // 32) * 32

        split_at = place()
        zone_b = sb("zone_b", NT, 2, S)
        ring = sb("ring", SLOTS, SLOT)
        gsel_at = place()
        h_hi = sb("h_hi", 2, 2, S, dt=F32R)
        h_lo = sb("h_lo", 2, 2, S, dt=F32R)
        gsel = nc.alloc_sbuf_tensor_at("gsel", [P, 2 * NE * ROUND], F32, offset=gsel_at)
        x_hi = nc.alloc_sbuf_tensor_at("x_hi", [P, KC, S], F32R, offset=split_at)
        x_lo = nc.alloc_sbuf_tensor_at("x_lo", [P, KC, S], F32R, offset=split_at + 4 * KC * S)
        h = sb("h", TT, D)
        hs = sb("hs", TT, D)
        yT_at = place()
        yT = sb("yT", KC, S)
        xT = sb("xT", KC, S)
        sb("w_lo_end", STAGES * SLOT - 2 * KC * S)
        memT = sb("memT", KC, S)
        ckv_at = place()
        ckv = sb("ckv", 2, 2048)
        sb("w_hi_end", STAGES * SLOT - 2 * 2048)
        w_hi = nc.alloc_sbuf_tensor_at("w_hi", [P, STAGES, SLOT], F32R, offset=ckv_at)
        w_lo = nc.alloc_sbuf_tensor_at("w_lo", [P, STAGES, SLOT], F32R, offset=yT_at)
        y_lo = nc.alloc_sbuf_tensor_at("y_lo", [P, KC, S], F32R, offset=yT_at)
        consts = sb("consts", CONST_W)
        rows_in = sb("rows_in", P)
        ldt = sb("ldt", DEPTH, NT)
        cols = sb("cols", P + DEPTH * NT)
        braw = sb("braw", 2, NT, 16)
        craw = sb("craw", 2, 2, 2, 64)
        wglu = sb("wglu", 2, 256)
        wrt = sb("wrt", KC, NE)
        sp = sb("sp", 20, DEPTH * NT)
        stat = sb("stat", 64)
        flag = sb("flag", 1, dt=I32)
        rot_tab = sb("rot_tab", 2, NT, S)
        zone_s = sb("zone_s", 6144)
        ptmp = sb("ptmp", 2, S)
        eps = sb("eps", 2)
        cstat = sb("cstat", 4)

        def c(name):
            return consts[:, CONST[name][0]:CONST[name][1]]

        ident, ones = c("ident"), c("ones")

        def col(name, l, i):
            r = ROW[name, l] + i
            return cols[:, r:r + 1]

        kT = ckv[:, 0, :].rearrange("p (c s) -> p c s", c=KC)
        vr = ckv[:, 1, :].rearrange("p (t d) -> p t d", t=TT)
        rqkT = ckv[:, 0, 0:1024].rearrange("p (c s) -> p c s", c=4)
        rvg = ckv[:, 0, 1024:2048].rearrange("p (t d) -> p t d", t=TT)
        rsc = ckv[:, 1, 0:768].rearrange("p (b s) -> p b s", b=2)
        ro = ckv[:, 1, 768:1280].rearrange("p (t d) -> p t d", t=TT)
        ro2 = ckv[:, 1, 1280:1792].rearrange("p (t d) -> p t d", t=TT)
        rqk = yT[:, 4:8, :].rearrange("p (t q) s -> p t (q s)", t=TT)
        rtmp = yT[:, 0:2, :].rearrange("p (x q) s -> p x (q s)", x=2)
        sqT = zone_s[:, 0:1024].rearrange("p (c s) -> p c s", c=4)
        skT = zone_s[:, 1024:2048].rearrange("p (c s) -> p c s", c=4)
        sv = zone_s[:, 2048:3072].rearrange("p (t d) -> p t d", t=TT)
        sa = zone_s[:, 3072:3840].rearrange("p (b s) -> p b s", b=2)
        slf = xT[:, 0:3, :].rearrange("p c s -> p (c s)").rearrange("p (b s) -> p b s", b=2)
        sw = xT[:, 3:6, :].rearrange("p c s -> p (c s)").rearrange("p (b s) -> p b s", b=2)
        uT = zone_s[:, 3840:4352].rearrange("p (c s) -> p c s", c=2)
        bb = zone_s[:, 4352:4864].rearrange("p (r i x) -> p r i x", r=2, i=NT)
        BT = zone_s[:, 4864:5376].rearrange("p (f r s) -> p f r s", f=2, r=2)
        CT = zone_s[:, 5376:5888].rearrange("p (f r s) -> p f r s", f=2, r=2)
        bbt = zone_s[:, 5888:6144].rearrange("p (r i x) -> p r i x", r=2, i=NT)
        yin = hs[:, 0, :].rearrange("p (r i s) -> p r i s", r=2, i=2)
        ysc = hs[:, 1, :].rearrange("p (r i s) -> p r i s", r=2, i=2)
        vtmp = yT[:, 2:4, :]
        rot_tmps = [x.rearrange("p (x i s) -> p x i s", x=2, i=NT) for x in (ckv[:, 1, :], zone_s[:, 1536:3584])]
        gT = zone_b[:, 0]
        glu_s = zone_b[:, 1]
        sq_a = zone_b[:, 2]
        sq_c = zone_b[:, 4:6].rearrange("p i r s -> p (i r) s")
        rstd_a = zone_b[:, 3, 0]
        rstd_c = zone_b[:, 3, 1]
        cqT = hs[:, :, :].rearrange("p t (c s) -> p (t c) s", c=4)
        cp = zone_b[:, 4:6].rearrange("p i r s -> p i r s")
        cpT = zone_b[:, 6:8]
        sg = zone_s[:, 0:512].rearrange("p (b s) -> p b s", b=2)
        hh = zone_s[:, 512:1536].rearrange("p (b t s) -> p b t s", b=2, t=2)
        sel = rot_tab[:, 0].rearrange("p i s -> p (i s)")
        scT = rot_tab[:, 1].rearrange("p i s -> p (i s)")
        xg = zone_s[:, 2560:3584].rearrange("p (c s) -> p c s", c=KC)
        ye = zone_s[:, 3584:4608]
        sc_cur = zone_s[:, 4608:4864]
        rt = zone_s[:, 4864:5888].rearrange("p (n x) -> p n x", n=64)
        fin_w = zone_s[:, 1536:2560]
        sqj = zone_s[:, 0:1024]

        landed = [sem(f"slot{s}_landed") for s in range(SLOTS)]
        bank_filled = [sem(f"bank{b}_filled") for b in range(8)]
        bank_free = [sem(f"bank{b}_free") for b in range(8)]
        consts_in, x_in, mem_in, rows_landed, ssm_in, router_in, finw_in, out_done = (
            sem(n) for n in ("consts_in", "x_in", "mem_in", "rows_landed", "ssm_in", "router_in", "finw_in", "out_done"))
        dve_step, act_step, pool_step = sem("dve_step"), sem("act_step"), sem("pool_step")
        names = ("eps_ready rstd_ready hs_ready sp_dt sp_range sp_sin sp_ready bb_ready rot_ready yin_im ysc_ready "
                 "x_re x_im rqk_ready rgn_sq rgn_rstd yb_ready sa_ready slf_ready sw_ready gelu_ready glu_ready sqa_ready "
                 "sqc_ready rstda rstdc ya_T yc_T cs_max cp_exp cp_ready gate_exp gate_in sel_ready gsel_ready mask_ready "
                 "flag_ready sg_ready sc_ready h_final final_ready ring_read hi_ready lo_ready stage_read xT_hi xT_lo hT_hi hT_lo xg_raw "
                 "attn_w_hi attn_w_lo attn_w_read attn_x_hi attn_x_lo").split()
        s = {n: sem(n) for n in names}

        def bank(key):
            return ps[:, uses[key][0], :]

        def wait_filled(eng, *key, e=None):
            b, n = uses[key]
            eng.wait_ge(bank_filled[b], n + 1 if e is None else e * per_expert[b] + (n + 1))

        def wait_taken(eng, *key, e=None):
            b, n = uses[key]
            eng.wait_ge(bank_free[b], n + 1 if e is None else e * per_expert[b] + (n + 1))

        def free(ins, *key):
            ins.then_inc(bank_free[uses[key][0]], 1)

        class Chain:

            def __init__(self, eng, sem_, base=0):
                self.eng, self.sem, self.n = eng, sem_, base

            def do(self, ins):
                ins.then_inc(self.sem, 1)
                self.n += 1
                self.settle()

            def settle(self):
                self.eng.wait_ge(self.sem, self.n)

        release, reads = {}, 0
        for k in jobs:
            name, l = k[0], k[1]
            if name == "in_u":
                release[k] = ("u", l)
            elif name == "in" and k[2] in ("sq", "sk"):
                release[k] = (k[2], l, 1)
            elif name == "kv" and k[2] < 2:
                release[k] = ("kT", l, 2 * k[2] + 1)
            elif name in ("q", "o"):
                release[k] = None
            elif name == "kv":
                release[k] = ("v", l, k[2] - 2, 1)
            elif name in ("in", "out"):
                if k[3] < 3:
                    reads += 1
                    release[k] = reads
                elif name == "in":
                    release[k] = (k[2], l, 1)
                else:
                    release[k] = (name, l, k[2], 1)

        attn_jobs = [k for k in jobs if k[0] in ("q", "o")]
        attn_stage, n_read = [], 0
        for k in attn_jobs:
            if k[3] < 3:
                n_read += 1
                attn_stage.append(n_read)
            else:
                attn_stage.append(("q", k[1], 2 * k[2] + 1) if k[0] == "q" else ("o", k[1], k[2], 1))

        def attn_pair(m):
            return w_hi[:, STAGES - 2 + m % 2, :], w_lo[:, STAGES - 2 + m % 2, :]

        def dense_no(k):
            return job_no[k] - job_no["dense_gu", 0, 0]

        def stage_release(blocks, fill_gu, fill_down):
            out, n = [], 0
            for k in blocks:
                if k[0].endswith("_gu") and k[2] == 3:
                    out.append(fill_gu(k[1]))
                elif k[0].endswith("_down") and k[1:] == (NJ - 1, 1):
                    out.append(fill_down)
                else:
                    n += 1
                    out.append(n)
            return out, n

        dense_jobs = [k for k in jobs if k[0].startswith("dense")]
        dense_stage, READS = stage_release(dense_jobs, lambda j: ("gu", j, 1), ("down", 3))

        def source(job):
            name = job[0]
            if name == "in_u":
                return a["w_in"][job[1], 512 * job[3]:512 * job[3] + 512, 0:256].rearrange("(k p) n -> p k n", p=P)
            if name == "in":
                o = IN_COLS[job[2]]
                w = a["w_in"][job[1], :, o:o + 512]
            elif name == "kv":
                w = a["w_cross_kv"][job[1], :, job[2] * 512:job[2] * 512 + 512]
            elif name in ("out", "q", "o"):
                w = a[{"out": "w_out", "q": "w_cross_q", "o": "w_cross_o"}[name]][job[1], :, job[2] * 512:job[2] * 512 + 512]
            elif name == "dense_gu":
                w = a["w_dense_gu"][0].rearrange("(k p) (g f) -> p k g f", p=P, g=2)
                return w[:, 2 * job[2]:2 * job[2] + 2, :, 256 * job[1]:256 * job[1] + 256]
            elif name == "dense_down":
                r = 256 * job[1] + P * job[2]
                return a["w_dense_down"][0, r:r + P, :]
            w = w.rearrange("(k p) n -> p k n", p=P)
            return w[:, 2 * job[3]:2 * job[3] + 2, :]

        def slot_of(n):
            return ring[:, n % SLOTS, :]

        def start_load(sp_, n, src):
            dst = slot_of(n)
            if len(src.shape) == 4:
                dst = dst.rearrange("p (k g f) -> p k g f", k=2, g=2)
                for g in range(2):
                    sp_.dma_start(dst[:, :, g, :], src[:, :, g, :]).then_inc(landed[n % SLOTS], 16)
            else:
                if len(src.shape) == 3:
                    dst = dst.rearrange("p (k n) -> p k n", k=src.shape[1])
                sp_.dma_start(dst, src).then_inc(landed[n % SLOTS], 16)

        def parts(key):
            return 2 if key[0].endswith("_gu") else 1

        landed_at, total = {}, [0] * SLOTS
        for n, k in enumerate(jobs):
            total[n % SLOTS] += 16 * parts(k)
            landed_at[n] = total[n % SLOTS]
        e_landed, e_total = {}, [0] * SLOTS
        for i, k in enumerate(expert_jobs):
            e_total[(BASE + i) % SLOTS] += 16 * parts(k)
            e_landed[i] = total[(BASE + i) % SLOTS] + e_total[(BASE + i) % SLOTS]

        def stage_free(eng, what, e=None, r=0):
            if isinstance(what, int):
                eng.wait_ge(s["stage_read"], what if e is None else e * READS + (READS * (1 + NE * r) + what))
            else:
                wait_filled(eng, *what, e=e)

        def experts(eng, order, do, ahead):
            items = schedule(order)

            def body(e, first, last):
                mine = [(at, what, j, 0) for at, what, j in items
                        if 0 <= at < JOBS_E and not (first and what == "block" and j < ahead)]
                before = [(at - JOBS_E, what, j, -1) for at, what, j in items if at >= JOBS_E and not first]
                after = [(at + JOBS_E, what, j, 1) for at, what, j in items if at < 0 and not last]
                for _, what, j, d in sorted(mine + before + after, key=lambda x: x[0]):
                    do[what](e + d, j)
                if last:
                    for at, what, j in items:
                        if at >= JOBS_E:
                            do[what](e, j)

            body(0, True, False)
            with eng.Fori(1, NE - 1) as e:
                body(e, False, False)
            body(NE - 1, False, True)

        block = ctx.enter_context(nc.Block())

        @block.sync
        def _(sync):
            sync.dma_start(h[:, :, :], a["x"][0].rearrange("(t p) d -> p t d", p=P)).then_inc(x_in, 16)
            sync.dma_start(consts[:, :], a["consts"]).then_inc(consts_in, 16)
            for n, r in (("mix_norm_w", "mix_norm"), ("cross_norm_w", "cross_norm"), ("ffn_norm_w", "ffn_norm"),
                         ("mix_out_gain", "gain"), ("ssm_d", "ssm_d")):
                w = a[n].rearrange("l (r p) -> (l r) p", p=P)
                sync.dma_start(rows_in[ROW[r, 0]:ROW[r, 0] + w.shape[0], :], w).then_inc(rows_landed, 16)
            sync.dma_start(rows_in[ROW["mem_norm", 0]:ROW["mem_norm", 0] + 8, :],
                          a["mem_norm_w"].rearrange("(r p) -> r p", p=P)).then_inc(rows_landed, 16)
            sync.dma_start(rows_in[ROWS:P, :], a["consts"][0:P - ROWS, 0:P]).then_inc(rows_landed, 16)
            for n in range(2):
                start_load(sync, n, source(jobs[n]))
            sync.wait_ge(rows_landed, 16 * N_ROW_LOADS)
            for t in range(TT):
                sync.dma_start(memT[:, 4 * t:4 * t + 4, :].rearrange("p c s -> p (c s)"),
                               a["mem"][0, t * P:(t + 1) * P, :]).then_inc(mem_in, 16)
            for n in range(2, SLOTS):
                start_load(sync, n, source(jobs[n]))

            def wait_free(k):
                if k in dense_jobs:
                    sync.wait_ge(s["lo_ready"], dense_no(k) + 1)
                elif k in attn_jobs:
                    sync.wait_ge(s["attn_w_lo"], attn_jobs.index(k) + 1)
                elif isinstance(release[k], int):
                    sync.wait_ge(s["ring_read"], release[k])
                else:
                    wait_filled(sync, *release[k])

            for n in range(SLOTS, BASE):
                wait_free(jobs[n - SLOTS])
                start_load(sync, n, source(jobs[n]))

            def expert_source(i, e):
                k = expert_jobs[i]
                one = isinstance(e, int)
                if k[0] == "expert_gu":
                    w = a["w_expert_gu"][0].rearrange("e (k p) (g f) -> p e k g f", p=P, g=2)
                    kk, f = slice(2 * k[2], 2 * k[2] + 2), slice(256 * k[1], 256 * k[1] + 256)
                    return w[:, e, kk, :, f] if one else w[:, bass.ds(e, 1), kk, :, f].rearrange("p e k g f -> p (e k) g f")
                w = a["w_expert_down"][0].rearrange("e (j k p) n -> p e j k n", p=P, k=2)
                return w[:, e, k[1], k[2]] if one else w[:, bass.ds(e, 1), k[1], k[2]]

            def expert_round(r):
                def split(e, i):
                    sync.wait_ge(s["lo_ready"], e * JOBS_E + (JOBS_E * (1 + NE * r) + i + 1))

                for i in range(SLOTS):
                    if r == 0:
                        wait_free(jobs[BASE - SLOTS + i])
                    else:
                        split(0, i - SLOTS)
                    start_load(sync, BASE + i, expert_source(i, 0))
                with sync.Fori(0, NE - 1) as e:
                    for i in range(SLOTS, JOBS_E):
                        split(e, i - SLOTS)
                        start_load(sync, BASE + i, expert_source(i, e))
                    for i in range(SLOTS):
                        split(e, i + JOBS_E - SLOTS)
                        start_load(sync, BASE + i, expert_source(i, e + 1))
                for i in range(SLOTS, JOBS_E):
                    split(NE - 1, i - SLOTS)
                    start_load(sync, BASE + i, expert_source(i, NE - 1))

            expert_round(0)
            sync.wait_ge(s["flag_ready"], 1)
            more = sync.value_load(flag[0:1, 0:1], min_val=0, max_val=1)
            with sync.If(more):
                expert_round(1)
            sync.wait_ge(s["final_ready"], TT)
            sync.dma_start(out[0].rearrange("(t p) d -> p t d", p=P), hs[:, :, :]).then_inc(out_done, 16)
            sync.wait_ge(out_done, 16)

        @block.tensor
        def _(pe):
            seen = [0] * 8

            def claim(*key, e=None, again=False):
                b, n = uses[key]
                if e is None:
                    assert seen[b] == n, key
                    seen[b] += 1
                    if n:
                        pe.wait_ge(bank_free[b], n)
                else:
                    pe.wait_ge(bank_free[b], e * per_expert[b] + n)
                return ps[:, b, :]

            def done(mm, *key):
                mm.then_inc(bank_filled[uses[key][0]], 1)

            def arrived(key):
                n = job_no[key]
                pe.wait_ge(landed[n % SLOTS], landed_at[n])
                return slot_of(n)

            def split_block(n, i):
                pe.wait_ge(s["lo_ready"], n + 1)
                return w_hi[:, i % STAGES, :], w_lo[:, i % STAGES, :]

            def product3(dst, x, x_rest, w, w_rest, first, last):
                nc.tensor.matmul(dst, x, w, start=first, stop=False, skip_group_check=True)
                nc.tensor.matmul(dst, x_rest, w, start=False, stop=False, skip_group_check=True)
                return nc.tensor.matmul(dst, x, w_rest, start=False, stop=last, skip_group_check=True)

            def transposes_of_rows(l, which, src):
                for i in range(4):
                    bk = claim("normT", l, which, i)
                    for cc in range(2):
                        for t in range(TT):
                            o = cc * 256 + t * P
                            ch = 2 * i + cc
                            mm = nc.tensor.transpose(bk[:, o:o + P], src[:, t, ch * P:(ch + 1) * P], ident)
                    done(mm, "normT", l, which, i)

            def rows_product(keys, lhs, name, l, cb, kc=KC):
                banks = [claim(*k) for k in keys]
                for kq in range(4):
                    w = arrived((name, l, cb, kq)).rearrange("p (k n) -> p k n", k=2)
                    for t in range(TT):
                        for k in range(2):
                            kk = 2 * kq + k
                            mm = nc.tensor.matmul(banks[t], lhs[:, kk, t * P:(t + 1) * P], w[:, k, :],
                                                  start=(kk == 0), stop=(kk == KC - 1))
                        if kq == 3:
                            done(mm, *keys[t])
                    if kq < 3:
                        mm.then_inc(s["ring_read"], 1)

            def cols_part(key, i, rhs, name, l, cb):
                ws = [arrived((name, l, cb, kq)).rearrange("p (k n) -> p k n", k=2) for kq in range(4)]
                bk = claim(*key)
                for cc in range(2):
                    m = (2 * i + cc) * P
                    for kk in range(KC):
                        mm = nc.tensor.matmul(bk[:, cc * 256:cc * 256 + 256], ws[kk // 2][:, kk % 2, m:m + P],
                                              rhs[:, kk, :], start=(kk == 0), stop=(kk == KC - 1))
                done(mm, *key)

            def cols_product(keys, rhs, name, l, cb):
                for i, key in enumerate(keys):
                    cols_part(key, i, rhs, name, l, cb)

            def key_part(l, i):
                cols_part(("kT", l, i), i % 2, memT, "kv", l, i // 2)

            def value_part(l, cb, t):
                bk = claim("v", l, cb, t)
                for kk in range(KC):
                    w = arrived(("kv", l, 2 + cb, kk // 2)).rearrange("p (k n) -> p k n", k=2)
                    mm = nc.tensor.matmul(bk, memT[:, kk, t * P:(t + 1) * P], w[:, kk % 2, :], start=(kk == 0), stop=(kk == KC - 1))
                done(mm, "v", l, cb, t)

            def all_taken(*keys):
                for k in keys:
                    wait_taken(pe, *k)

            def xT_written(l, which):
                all_taken(*[("normT", l, which, i) for i in range(4)])

            pe.wait_ge(consts_in, 16)
            pe.wait_ge(rows_landed, 16 * N_ROW_LOADS)
            bk = claim("cols")
            nc.tensor.transpose(bk[:, 0:P], rows_in[:, :], ident)
            mm = nc.tensor.matmul(bk[:, P:P + DEPTH * NT], c("half")[0:2, :], ldt[0:2].rearrange("p l i -> p (l i)"),
                                  start=True, stop=True)
            done(mm, "cols")

            for l in range(DEPTH):
                pe.wait_ge(s["hs_ready"], 2 + 3 * l if l else 1)
                transposes_of_rows(l, "mix", hs)
                xT_written(l, "mix")
                w = [arrived(("in_u", l, 0, kh)).rearrange("p (k n) -> p k n", k=4) for kh in range(2)]
                bk = claim("u", l)
                for cc in range(2):
                    for k in range(KC):
                        mm = nc.tensor.matmul(bk[:, cc * 256:cc * 256 + 256], w[k // 4][:, k % 4, cc * P:(cc + 1) * P], xT[:, k, :],
                                              start=(k == 0), stop=(k == KC - 1))
                done(mm, "u", l)
                rows_product([("rqk", l, t) for t in range(TT)], xT, "in", l, "rqk")
                if l == 0:
                    pe.wait_ge(s["hs_ready"], 2)
                    transposes_of_rows("mem", 0, hs)
                pe.wait_ge(s["bb_ready"], l + 1)
                bk = claim("BT", l)
                for f in range(2):
                    for r in range(2):
                        o = (2 * f + r) * P
                        mm = nc.tensor.transpose(bk[:, o:o + P], bb[:, r, 4 * f:4 * f + 4, :].rearrange("p i x -> p (i x)"), ident)
                done(mm, "BT", l)
                pe.wait_ge(ssm_in, 16 * N_SSM_LOADS * (l + 1))
                bk = claim("CT", l)
                for f in range(2):
                    for r in range(2):
                        o = (2 * f + r) * P
                        mm = nc.tensor.transpose(bk[:, o:o + P], craw[:, f, r].rearrange("p a n -> p (a n)"), ident)
                done(mm, "CT", l)
                cols_product([("sq", l, 0), ("sq", l, 1)], xT, "in", l, "sq")
                all_taken(("u", l), ("BT", l))
                for i in range(NT):
                    bk = claim("bu", l, i)
                    q = 32 * (i % 4)
                    for r in range(2):
                        mm = nc.tensor.matmul(bk[:, 256 * r:256 * r + 256], BT[q:q + 32, i // 4, r, :], uT[q:q + 32, i // 4, :],
                                              start=True, stop=True)
                    done(mm, "bu", l, i)
                cols_product([("sk", l, 0), ("sk", l, 1)], xT, "in", l, "sk")
                rows_product([("rvg", l, t) for t in range(TT)], xT, "in", l, "rvg")
                rows_product([("sv", l, t) for t in range(TT)], xT, "in", l, "sv")
                pe.wait_ge(s["rqk_ready"], l + 1)
                for w_ in range(2):
                    bk = claim("rT", l, w_)
                    for cc in range(2):
                        for t in range(TT):
                            o = cc * 256 + t * P
                            mm = nc.tensor.transpose(bk[:, o:o + P], rqk[:, t, 256 * w_ + cc * P:256 * w_ + (cc + 1) * P], ident)
                    done(mm, "rT", l, w_)
                all_taken(("rT", l, 0), ("rT", l, 1), ("rvg", l, 0), ("rvg", l, 1))
                ob = claim("ro", l)

                def ret_scores(hd):
                    bk = claim("rs", l, hd)
                    p0, cc = DH * (hd % 2), hd // 2
                    nc.tensor.matmul(bk[:, 0:256], rqkT[p0:p0 + DH, 2 + cc, 0:P], rqkT[p0:p0 + DH, cc, :], start=True, stop=True)
                    mm = nc.tensor.matmul(bk[:, 256:384], rqkT[p0:p0 + DH, 2 + cc, P:256], rqkT[p0:p0 + DH, cc, P:256],
                                          start=True, stop=True)
                    done(mm, "rs", l, hd)

                def ret_out(hd):
                    wait_taken(pe, "rs", l, hd)
                    sc, o = rsc[:, hd % 2], DH * hd
                    nc.tensor.matmul(ob[:, o:o + DH], sc[:, 0:P], rvg[:, 0, o:o + DH], start=True, stop=True)
                    nc.tensor.matmul(ob[:, 256 + o:256 + o + DH], sc[:, P:256], rvg[:, 0, o:o + DH], start=True, stop=False)
                    return nc.tensor.matmul(ob[:, 256 + o:256 + o + DH], sc[:, 256:384], rvg[:, 1, o:o + DH],
                                            start=False, stop=True)

                for hd in range(RH):
                    ret_scores(hd)
                    if hd:
                        ret_out(hd - 1)
                done(ret_out(RH - 1), "ro", l)
                all_taken(*[(n, l, i) for n in ("sq", "sk", "sv") for i in range(2)])
                for step in range(SH + 2):
                    if step < SH:
                        hd = step
                        bk = claim("sz", l, hd)
                        p0, cc = DH * (hd % 2), hd // 2
                        nc.tensor.matmul(bk[:, 0:256], skT[p0:p0 + DH, cc, 0:P], sqT[p0:p0 + DH, cc, :], start=True, stop=True,
                                         skip_group_check=True)
                        mm = nc.tensor.matmul(bk[:, 256:384], skT[p0:p0 + DH, cc, P:256], sqT[p0:p0 + DH, cc, P:256],
                                              start=False, stop=True, skip_group_check=True)
                        done(mm, "sz", l, hd)
                    if step in FILLERS:
                        if step == 0:
                            xT_written("mem", 0)
                        key_part(l, FILLERS.index(step))
                    if 1 <= step <= SH:
                        hd = step - 1
                        bk = claim("sc", l, hd)
                        pe.wait_ge(s["slf_ready"], SH * l + hd + 1)
                        lf = slf[:, hd % 2]
                        nc.tensor.matmul(bk[:, 0:256], c("tri_ge"), lf[:, 0:256], start=False, stop=True, skip_group_check=True)
                        nc.tensor.matmul(bk[:, P:256], ones, lf[:, 256:384], start=False, stop=True, skip_group_check=True)
                        mm = nc.tensor.matmul(bk[:, 256:384], c("tri_ge"), lf[:, 256:384], start=False, stop=True,
                                              skip_group_check=True)
                        done(mm, "sc", l, hd)
                    if step >= 2:
                        hd = step - 2
                        if hd % 4 == 0:
                            so = claim("so", l, hd // 4)
                        pe.wait_ge(s["sw_ready"], SH * l + hd + 1)
                        w = sw[:, hd % 2]
                        p0, o = DH * (hd % 2), 256 * (hd // 2 % 2)
                        vv = slice(DH * hd, DH * hd + DH)
                        nc.tensor.matmul(so[p0:p0 + DH, o:o + 256], sv[:, 0, vv], w[:, 0:256], start=True, stop=False,
                                         skip_group_check=True)
                        mm = nc.tensor.matmul(so[p0:p0 + DH, o + P:o + 256], sv[:, 1, vv], w[:, 256:384], start=False, stop=True,
                                              skip_group_check=True)
                        if hd % 4 == 3:
                            done(mm, "so", l, hd // 4)
                pe.wait_ge(s["yb_ready"], l + 1)
                bk = claim("ybT", l)
                for cc in range(2):
                    for t in range(TT):
                        o = cc * 256 + t * P
                        mm = nc.tensor.transpose(bk[:, o:o + P], ro[:, t, cc * P:(cc + 1) * P], ident)
                done(mm, "ybT", l)
                wait_taken(pe, "CT", l)
                bk = claim("y", l)
                for i in range(NT):
                    if i % 2 == 0:
                        pe.wait_ge(s["x_re"], 4 * l + i // 2 + 1)
                        pe.wait_ge(s["x_im"], 4 * l + i // 2 + 1)
                    q = 32 * (i % 4)
                    for r in range(2):
                        mm = nc.tensor.matmul(bk[q:q + 32, 256 * (i // 4):256 * (i // 4) + 256], CT[:, i // 4, r, q:q + 32],
                                              zone_b[:, i, r, :], start=(r == 0), stop=(r == 1), skip_group_check=True)
                done(mm, "y", l)
                key_part(l, 3)
                pe.wait_ge(s["gelu_ready"], l + 1)
                bk = claim("glu", l)
                for m in range(2):
                    for k in range(2):
                        mm = nc.tensor.matmul(bk[:, 256 * m:256 * m + 256], wglu[:, k, P * m:P * m + P], gT[:, k, :],
                                              start=(k == 0), stop=(k == 1))
                done(mm, "glu", l)
                value_part(l, 0, 0)
                for key, ready, sq, n in (("ssa", "sqa_ready", sq_a, 2), ("ssc", "sqc_ready", sq_c, 4)):
                    pe.wait_ge(s[ready], l + 1)
                    bk = claim(key, l)
                    for k in range(n):
                        mm = nc.tensor.matmul(bk[:, 0:256], ones, sq[:, k, :], start=(k == 0), stop=(k == n - 1))
                    done(mm, key, l)
                value_part(l, 0, 1)
                pe.wait_ge(s["ya_T"], l + 1)
                wait_taken(pe, "ybT", l)
                pe.wait_ge(s["yc_T"], l + 1)
                for cb in range(2):
                    rows_product([("out", l, cb, t) for t in range(TT)], yT, "out", l, cb)
                for t in range(TT):
                    value_part(l, 1, t)

                pe.wait_ge(s["hs_ready"], 3 + 3 * l)
                transposes_of_rows(l, "cross", hs)
                for cb in range(2):
                    banks = [claim("q", l, 2 * cb + i) for i in range(2)]
                    for kq in range(4):
                        m = attn_jobs.index(("q", l, cb, kq))
                        pe.wait_ge(s["attn_w_lo"], m + 1)
                        w, w_rest = (x.rearrange("p (k n) -> p k n", k=2) for x in attn_pair(m))
                        if cb == 0:
                            pe.wait_ge(s["attn_x_hi"], 8 * l + kq + 1)
                            pe.wait_ge(s["attn_x_lo"], 8 * l + kq + 1)
                        for c_ in range(4):
                            cs_, dst = slice(c_ * P, (c_ + 1) * P), banks[c_ // 2][:, 256 * (c_ % 2):256 * (c_ % 2) + 256]
                            for k in range(2):
                                kk = 2 * kq + k
                                mm = product3(dst, w[:, k, cs_], w_rest[:, k, cs_], x_hi[:, kk, :], x_lo[:, kk, :],
                                              kk == 0 and c_ % 2 == 0, kk == KC - 1)
                            if kq == 3 and c_ % 2:
                                done(mm, "q", l, 2 * cb + c_ // 2)
                        if kq < 3:
                            mm.then_inc(s["attn_w_read"], 1)
                all_taken(*[(n, l, i) for n in ("q", "kT") for i in range(4)])
                all_taken(*[("v", l, cb, t) for cb in range(2) for t in range(TT)])

                def cross_scores(hd):
                    bk = claim("cs", l, hd)
                    for t in range(TT):
                        for k in range(2):
                            mm = nc.tensor.matmul(bk[:, 256 * t:256 * t + 256], cqT[:, 2 * hd + k, t * P:(t + 1) * P],
                                                  kT[:, 2 * hd + k, :], start=(k == 0), stop=(k == 1))
                    done(mm, "cs", l, hd)

                def cross_out(hd):
                    pe.wait_ge(s["cp_ready"], CH * l + hd + 1)
                    bk = claim("cp", l, hd)
                    for m in range(2):
                        for t in range(TT):
                            o = 256 * m + t * P
                            mm = nc.tensor.transpose(bk[:, o:o + P], cp[:, hd % 2, t, m * P:(m + 1) * P], ident)
                    done(mm, "cp", l, hd)
                    wait_taken(pe, "cp", l, hd)
                    bk = claim("co", l, hd)
                    for cc in range(2):
                        for m in range(2):
                            ch = (2 * hd + cc) * P
                            mm = nc.tensor.matmul(bk[:, 256 * cc:256 * cc + 256], vr[:, m, ch:ch + P], cpT[:, hd % 2, m, :],
                                                  start=(m == 0), stop=(m == 1))
                    done(mm, "co", l, hd)

                for hd in range(CH):
                    cross_scores(hd)
                    if hd:
                        cross_out(hd - 1)
                cross_out(CH - 1)
                for cb in range(2):
                    banks = [claim("o", l, cb, t) for t in range(TT)]
                    for kq in range(4):
                        m = attn_jobs.index(("o", l, cb, kq))
                        pe.wait_ge(s["attn_w_lo"], m + 1)
                        w, w_rest = (x.rearrange("p (k n) -> p k n", k=2) for x in attn_pair(m))
                        if cb == 0:
                            pe.wait_ge(s["attn_x_hi"], 8 * l + 4 + kq + 1)
                            pe.wait_ge(s["attn_x_lo"], 8 * l + 4 + kq + 1)
                        for t in range(TT):
                            ts = slice(t * P, (t + 1) * P)
                            for k in range(2):
                                kk = 2 * kq + k
                                mm = product3(banks[t], x_hi[:, kk, ts], y_lo[:, kk, ts], w[:, k, :], w_rest[:, k, :],
                                              kk == 0, kk == KC - 1)
                            if kq == 3:
                                done(mm, "o", l, cb, t)
                        if kq < 3:
                            mm.then_inc(s["attn_w_read"], 1)

                pe.wait_ge(s["hs_ready"], 4 + 3 * l)
                transposes_of_rows(l, "ffn", hs)
                if l:
                    xT_written(l, "ffn")
                else:
                    def turn(j):
                        for t in range(TT):
                            wait_taken(pe, "gu", j, t)
                            bk = claim("hT", j, t)
                            for k in range(2):
                                mm = nc.tensor.transpose(bk[:, k * P:(k + 1) * P], hh[:, j % 2, t, k * P:(k + 1) * P], ident)
                            done(mm, "hT", j, t)

                    for step in range(NJ + 2):
                        if step < NJ:
                            banks = [claim("gu", step, t) for t in range(TT)]
                            for kq in range(4):
                                n = dense_no(("dense_gu", step, kq))
                                w, w_rest = (x.rearrange("p (k n) -> p k n", k=2) for x in split_block(n, n))
                                if step == 0:
                                    pe.wait_ge(s["xT_hi"], kq + 1)
                                    pe.wait_ge(s["xT_lo"], kq + 1)
                                for t in range(TT):
                                    ts = slice(t * P, (t + 1) * P)
                                    for k in range(2):
                                        kk = 2 * kq + k
                                        mm = product3(banks[t], x_hi[:, kk, ts], x_lo[:, kk, ts], w[:, k, :], w_rest[:, k, :],
                                                      kk == 0, kk == KC - 1)
                                    if kq == 3:
                                        done(mm, "gu", step, t)
                                if kq < 3:
                                    mm.then_inc(s["stage_read"], 1)
                        if step == NJ:
                            turn(NJ - 1)
                        if step >= 2:
                            j = step - 2
                            if j == 0:
                                down = [claim("down", b) for b in range(4)]
                            pe.wait_ge(s["hT_hi"], 2 * j + 2)
                            pe.wait_ge(s["hT_lo"], 2 * j + 2)
                            for k in range(2):
                                n = dense_no(("dense_down", j, k))
                                w, w_rest = split_block(n, n)
                                for b in range(4):
                                    ts, ns = slice(b // 2 * P, b // 2 * P + P), slice(512 * (b % 2), 512 * (b % 2) + 512)
                                    mm = product3(down[b], h_hi[:, j % 2, k, ts], h_lo[:, j % 2, k, ts], w[:, ns], w_rest[:, ns],
                                                  j == 0 and k == 0, j == NJ - 1 and k == 1)
                                    if (j, k) == (NJ - 1, 1):
                                        done(mm, "down", b)
                                if (j, k) != (NJ - 1, 1):
                                    mm.then_inc(s["stage_read"], 1)
                        if 1 <= step < NJ:
                            turn(step - 1)

            pe.wait_ge(router_in, 16)
            bk = claim("logits")
            for t in range(TT):
                for k in range(KC):
                    mm = nc.tensor.matmul(bk[:, 8 * t:8 * t + 8], xT[:, k, t * P:(t + 1) * P], wrt[:, k, :],
                                          start=(k == 0), stop=(k == KC - 1))
            done(mm, "logits")
            pe.wait_ge(s["mask_ready"], 1)
            bk = claim("rank")
            mask = rt[:, 0]
            nc.tensor.matmul(bk[:, 0:8], c("tri_lt"), mask[:, 0:8], start=True, stop=True)
            nc.tensor.matmul(bk[:, 8:16], c("tri_lt"), mask[:, 8:16], start=True, stop=False)
            nc.tensor.matmul(bk[:, 8:16], ones, mask[:, 0:8], start=False, stop=True)
            nc.tensor.matmul(bk[:, 16:24], ones, mask[:, 0:8], start=True, stop=False)
            mm = nc.tensor.matmul(bk[:, 16:24], ones, mask[:, 8:16], start=False, stop=True)
            done(mm, "rank")

            def expert_round(r):
                first = JOBS_E * (1 + NE * r)
                rows = NJ * (2 + NE * r)

                def gather(e):
                    for i in range(2):
                        bk = claim("xg", r, i, e=e)
                        for x in range(4):
                            ch = 4 * i + x
                            for t in range(TT):
                                mm = nc.tensor.matmul(bk[:, x * P:(x + 1) * P], hs[:, t, ch * P:(ch + 1) * P],
                                                      sel[:, bass.ds(e * 256 + t * P, P)], start=(t == 0), stop=(t == 1))
                        done(mm, "xg", r, i)

                def gate_up(e, step):
                    bk = claim("egu", r, step, e=e)
                    for kq in range(4):
                        i = ejob_no["expert_gu", step, kq]
                        w, w_rest = (x.rearrange("p (k n) -> p k n", k=2) for x in split_block(e * JOBS_E + (first + i), i))
                        for k in range(2):
                            kk = 2 * kq + k
                            mm = product3(bk, x_hi[:, kk, 0:P], x_lo[:, kk, 0:P], w[:, k, :], w_rest[:, k, :],
                                          kk == 0, kk == KC - 1)
                        if kq < 3:
                            mm.then_inc(s["stage_read"], 1)
                    done(mm, "egu", r, step)

                def down(e, j):
                    for k in range(2):
                        i = ejob_no["expert_down", j, k]
                        w, w_rest = split_block(e * JOBS_E + (first + i), i)
                        if k == 0:
                            pe.wait_ge(s["hT_hi"], e * NJ + (rows + j + 1))
                            pe.wait_ge(s["hT_lo"], e * NJ + (rows + j + 1))
                        for n in range(2):
                            bk = claim("ey", r, n, e=e) if (j, k) == (0, 0) else bank(("ey", r, n))
                            ns = slice(512 * n, 512 * n + 512)
                            mm = product3(bk, h_hi[:, j % 2, k, 0:P], h_lo[:, j % 2, k, 0:P], w[:, ns], w_rest[:, ns],
                                          j == 0 and k == 0, j == NJ - 1 and k == 1)
                            if (j, k) == (NJ - 1, 1):
                                done(mm, "ey", r, n)
                        if (j, k) != (NJ - 1, 1):
                            mm.then_inc(s["stage_read"], 1)

                def turn(e, j):
                    wait_taken(pe, "egu", r, j, e=e)
                    bk = claim("ehT", r, j, e=e)
                    for k in range(2):
                        mm = nc.tensor.transpose(bk[:, k * P:(k + 1) * P], hh[:, j % 2, 0, k * P:(k + 1) * P], ident)
                    done(mm, "ehT", r, j)

                def scatter(e):
                    for n in range(2):
                        wait_taken(pe, "ey", r, n, e=e)
                    pe.wait_ge(s["sc_ready"], e + (1 + r * NE))
                    for i in range(4):
                        t, n = i // 2, i % 2
                        bk = claim("eo", r, i, e=e)
                        mm = nc.tensor.matmul(bk, sc_cur[:, t * P:(t + 1) * P], ye[:, 512 * n:512 * n + 512],
                                              start=True, stop=True)
                        done(mm, "eo", r, i)

                def gathered(e):
                    pe.wait_ge(s["xT_hi"], e + (5 + r * NE))
                    pe.wait_ge(s["xT_lo"], e + (5 + r * NE))

                def expert(e, last):
                    for step in range(1, NJ):
                        gate_up(e, step)
                        if step >= 2:
                            down(e, step - 2)
                        turn(e, step - 1)
                    if not last:
                        gather(e + 1)
                    turn(e, NJ - 1)
                    down(e, NJ - 2)
                    down(e, NJ - 1)
                    if not last:
                        gathered(e + 1)
                        gate_up(e + 1, 0)
                    scatter(e)

                pe.wait_ge(s["sel_ready"], r + 1)
                gather(0)
                pe.wait_ge(s["gsel_ready"], r + 1)
                for i in range(4):
                    bk = claim("scT", r, i)
                    for x in range(4):
                        o = (4 * i + x) * P
                        mm = nc.tensor.transpose(bk[:, x * P:(x + 1) * P], gsel[:, o:o + P], ident)
                    done(mm, "scT", r, i)
                gathered(0)
                gate_up(0, 0)
                with pe.Fori(0, NE - 1) as e:
                    expert(e, False)
                expert(NE - 1, True)

            expert_round(0)
            for b in range(8):
                seen[b] = min(n for k, (bb_, n) in uses.items() if bb_ == b and k[0] in ("scT", "xg", "egu", "ehT", "ey", "eo") and k[1] == 1)
            pe.wait_ge(s["flag_ready"], 1)
            more = pe.value_load(flag[0:1, 0:1], min_val=0, max_val=1)
            with pe.If(more):
                expert_round(1)

        @block.scalar
        def _(act):
            ch = Chain(act, act_step)
            for l in range(DEPTH):
                for n, r in ((("ssm_lambda_re", "lam_re")), ("ssm_lambda_im", "lam_im")):
                    act.dma_start(rows_in[ROW[r, l]:ROW[r, l] + 8, :],
                                  a[n][l].rearrange("(i g) n -> i (g n)", g=2)).then_inc(rows_landed, 16)
                act.dma_start(ldt[0:2, l].rearrange("g (i o) -> g i o", o=1),
                              a["ssm_log_dt"][l].rearrange("(i g o) -> g i o", g=2, o=1), allow_slow_non_contiguous=True).then_inc(rows_landed, 16)
            def load_ssm(l):
                for r, n in enumerate(("ssm_b_re", "ssm_b_im")):
                    act.dma_start(braw[:, r], a[n][l].rearrange("(i g) n x -> (g n) i x", g=2)).then_inc(ssm_in, 16)
                for r, n in enumerate(("ssm_c_re", "ssm_c_im")):
                    w = a[n][l].rearrange("(f g) x n -> (g x) f n", f=2)
                    for dup in range(2):
                        act.dma_start(craw[:, :, r, dup, :], w).then_inc(ssm_in, 16)
                act.dma_start(wglu[:, :, :], a["ssm_w_glu"][l].rearrange("(k p) n -> p k n", p=P)).then_inc(ssm_in, 16)

            norm_no = [0]

            def row_norm(src, after=None, l=None):
                n = norm_no[0]
                norm_no[0] += 1
                o = 4 * n
                ch.do(nc.scalar.activation(eps[:, 1:2], eps[:, 0:1], ACT.Ln))
                ch.settle()
                for t in range(TT):
                    for k in range(2):
                        if after == "down":
                            wait_taken(act, "down", 2 * t + k)
                        elif after:
                            wait_taken(act, after, l, k, t)
                    ch.do(nc.scalar.activation(sqj, src[:, t, :], ACT.Square, accum_out=stat[:, o + t:o + t + 1]))
                    ch.settle()
                ch.do(nc.scalar.activation(stat[:, o + 2:o + 4], stat[:, o:o + 2], ACT.Ln, bias=eps[:, 0:1], scale=1.0 / D))
                ch.settle()
                nc.scalar.activation(stat[:, o:o + 2], stat[:, o + 2:o + 4], ACT.Exp, scale=-0.5).then_inc(s["rstd_ready"], 1)

            act.wait_ge(s["eps_ready"], 1)
            act.wait_ge(x_in, 16)
            row_norm(h)
            load_ssm(0)
            act.dma_start(wrt[:, :, :], a["w_router"][0].rearrange("(k p) e -> p k e", p=P)).then_inc(router_in, 16)
            wait_taken(act, "cols")
            nc.scalar.activation(sp[:, 1, :], cols[:, P:P + DEPTH * NT], ACT.Exp).then_inc(s["sp_dt"], 1)
            act.wait_ge(s["sp_range"], 1)
            ch.do(nc.scalar.activation(sp[:, 4, :], sp[:, 2, :], ACT.Exp))
            ch.do(nc.scalar.activation(sp[:, 5, :], sp[:, 3, :], ACT.Sin))
            ch.do(nc.scalar.activation(sp[:, 6, :], sp[:, 3, :], ACT.Sin, scale=0.5))
            ch.settle()
            nc.scalar.copy(sp[:, 7, :], sp[:, 6, :]).then_inc(s["sp_sin"], 1)
            act.wait_ge(mem_in, 32)
            row_norm(memT.rearrange("p (t c) s -> p t (c s)", t=TT))

            for l in range(DEPTH):
                if l:
                    row_norm(h, "down")
                def evacuate(key, dst, scale=None):
                    wait_filled(act, *key)
                    if scale is None:
                        free(nc.scalar.copy(dst, bank(key)), *key)
                    else:
                        free(nc.scalar.mul(dst, bank(key), scale), *key)

                def two(dst, i):
                    return dst[:, 2 * i:2 * i + 2, :].rearrange("p c s -> p (c s)")

                evacuate(("u", l), uT.rearrange("p c s -> p (c s)"))
                for i in range(2):
                    evacuate(("sq", l, i), two(sqT, i), DH ** -0.5)
                for i in range(NT):
                    evacuate(("bu", l, i), zone_b[:, i].rearrange("p r s -> p (r s)"))
                if l:
                    act.wait_ge(s["rot_ready"], l + 1)
                for i in range(2):
                    evacuate(("sk", l, i), two(skT, i))
                for t in range(TT):
                    wait_filled(act, "rvg", l, t)
                    ch.do(nc.scalar.copy(rvg[:, t, 0:256], bank(("rvg", l, t))[:, 0:256]))
                    ch.settle()
                    free(nc.scalar.activation(rvg[:, t, 256:512], bank(("rvg", l, t))[:, 256:512], ACT.Silu), "rvg", l, t)
                for t in range(TT):
                    evacuate(("sv", l, t), sv[:, t, :])
                for w_ in range(2):
                    evacuate(("rT", l, w_), two(rqkT, w_))
                act.wait_ge(s["rgn_sq"], l + 1)
                ch.do(nc.scalar.activation(stat[:, 40:48], stat[:, 32:40], ACT.Ln, bias=eps[:, 0:1], scale=1.0 / DH))
                ch.settle()
                nc.scalar.activation(stat[:, 48:56], stat[:, 40:48], ACT.Exp, scale=-0.5).then_inc(s["rgn_rstd"], 1)

                for step in range(SH + 1):
                    if step < SH:
                        hd = step
                        wait_filled(act, "sz", l, hd)
                        t_ = sa[:, hd % 2]
                        if hd >= 2:
                            act.wait_ge(s["slf_ready"], SH * l + hd - 1)
                        ch.do(nc.scalar.activation(t_, bank(("sz", l, hd))[:, 0:384], ACT.Abs))
                        ch.settle()
                        ch.do(nc.scalar.activation(t_, t_, ACT.Exp, scale=-1.0))
                        ch.settle()
                        nc.scalar.activation(t_, t_, ACT.Ln, bias=1.0).then_inc(s["sa_ready"], 1)
                    if step >= 1:
                        hd = step - 1
                        wait_taken(act, "sc", l, hd)
                        nc.scalar.activation(sw[:, hd % 2], sw[:, hd % 2], ACT.Exp).then_inc(s["sw_ready"], 1)
                for i in range(2):
                    evacuate(("so", l, i), two(yT, 2 + i))

                def values(cb, t):
                    evacuate(("v", l, cb, t), vr[:, t, 512 * cb:512 * cb + 512])

                wait_filled(act, "y", l)
                for i in range(2):
                    wait_taken(act, "so", l, i)
                nc.scalar.activation(sq_c.rearrange("p c s -> p (c s)"), yT[:, 4:8, :].rearrange("p c s -> p (c s)"),
                                     ACT.Square).then_inc(s["sqc_ready"], 1)
                wait_taken(act, "y", l)
                nc.scalar.activation(gT.rearrange("p c s -> p (c s)"), glu_s.rearrange("p c s -> p (c s)"),
                                     ACT.Gelu_apprx_tanh).then_inc(s["gelu_ready"], 1)
                evacuate(("kT", l, 3), two(kT, 3))
                wait_filled(act, "glu", l)
                free(nc.scalar.activation(glu_s.rearrange("p c s -> p (c s)"), bank(("glu", l)), ACT.Sigmoid), "glu", l)
                if l + 1 < DEPTH:
                    load_ssm(l + 1)
                act.wait_ge(s["glu_ready"], l + 1)
                nc.scalar.activation(sq_a.rearrange("p c s -> p (c s)"), gT.rearrange("p c s -> p (c s)"),
                                     ACT.Square).then_inc(s["sqa_ready"], 1)
                values(0, 0)
                for key, n, dst, sig in (("ssa", 256, rstd_a, "rstda"), ("ssc", 512, rstd_c, "rstdc")):
                    wait_filled(act, key, l)
                    free(nc.scalar.activation(dst, bank((key, l))[:, 0:256], ACT.Ln, bias=eps[:, 0:1], scale=1.0 / n), key, l)
                    wait_taken(act, key, l)
                    nc.scalar.activation(dst, dst, ACT.Exp, scale=-0.5).then_inc(s[sig], 1)

                def attn_w_hi(m):
                    n = job_no[attn_jobs[m]]
                    act.wait_ge(landed[n % SLOTS], landed_at[n])
                    if m >= 2:
                        if isinstance(attn_stage[m - 2], int):
                            act.wait_ge(s["attn_w_read"], attn_stage[m - 2])
                        else:
                            wait_filled(act, *attn_stage[m - 2])
                    nc.scalar.copy(attn_pair(m)[0], slot_of(n)).then_inc(s["attn_w_hi"], 1)

                values(0, 1)
                q0, o0 = 16 * l, 16 * l + 8
                attn_w_hi(q0)
                attn_w_hi(q0 + 1)
                row_norm(h, "out", l)
                for t in range(TT):
                    values(1, t)
                for i in range(4):
                    wait_taken(act, "normT", l, "cross", i)
                    nc.scalar.copy(x_hi[:, 2 * i:2 * i + 2, :], xT[:, 2 * i:2 * i + 2, :]).then_inc(s["attn_x_hi"], 1)
                for m in range(2, 8):
                    attn_w_hi(q0 + m)
                    if m >= 5:
                        evacuate(("q", l, m - 5), two(cqT, m - 5), 256 ** -0.5)
                evacuate(("q", l, 3), two(cqT, 3), 256 ** -0.5)

                def attn_y_hi(hd):
                    wait_filled(act, "co", l, hd)
                    nc.scalar.copy(x_hi[:, 2 * hd:2 * hd + 2, :].rearrange("p c s -> p (c s)"),
                                   bank(("co", l, hd))).then_inc(s["attn_x_hi"], 1)

                for hd in range(CH):
                    act.wait_ge(s["cs_max"], CH * l + hd + 1)
                    if hd >= 2:
                        wait_filled(act, "cp", l, hd - 2)
                    for t in range(TT):
                        ch.do(nc.scalar.activation(cp[:, hd % 2, t, :], bank(("cs", l, hd))[:, 256 * t:256 * t + 256], ACT.Exp,
                                                   bias=stat[:, 56 + t:57 + t], accum_out=stat[:, 58 + t:59 + t]))
                    ch.settle()
                    nc.scalar.copy(stat[:, 63:64], stat[:, 61:62]).then_inc(s["cp_exp"], 1)
                    if hd:
                        attn_y_hi(hd - 1)
                    evacuate(("cp", l, hd), cpT[:, hd % 2].rearrange("p m s -> p (m s)"))
                    if hd >= 2:
                        attn_w_hi(o0 + hd - 2)
                attn_y_hi(CH - 1)
                for m in range(2, 8):
                    attn_w_hi(o0 + m)

                row_norm(h, "o", l)
                if l == 0:
                    def silu(j):
                        for t in range(TT):
                            if j:
                                wait_taken(act, "gu", j - 1, t)
                            wait_filled(act, "gu", j, t)
                            nc.scalar.activation(sg[:, t], bank(("gu", j, t))[:, 0:256], ACT.Silu).then_inc(s["sg_ready"], 1)

                    def hidden(j):
                        for t in range(TT):
                            wait_filled(act, "hT", j, t)
                            nc.scalar.copy(h_hi[:, j % 2, :, t * P:(t + 1) * P],
                                           bank(("hT", j, t))[:, 0:256].rearrange("p (k s) -> p k s", k=2)).then_inc(s["hT_hi"], 1)

                    def hi_block(i):
                        n = job_no[dense_jobs[i]]
                        act.wait_ge(landed[n % SLOTS], landed_at[n])
                        if i >= STAGES:
                            stage_free(act, dense_stage[i - STAGES])
                        nc.scalar.copy(w_hi[:, i % STAGES, :], slot_of(n)).then_inc(s["hi_ready"], 1)

                    for i in range(HI_AHEAD):
                        hi_block(i)
                    for i in range(4):
                        wait_taken(act, "normT", l, "ffn", i)
                        nc.scalar.copy(x_hi[:, 2 * i:2 * i + 2, :], xT[:, 2 * i:2 * i + 2, :]).then_inc(s["xT_hi"], 1)
                    for _, what, j in schedule(SCALAR_DENSE):
                        if what != "block" or j >= HI_AHEAD:
                            {"block": hi_block, "silu": silu, "hidden": hidden}[what](j)

            act.wait_ge(s["gate_in"], 1)
            nc.scalar.activation(rt[:, 2, 0:2], rt[:, 1, 0:2], ACT.Exp).then_inc(s["gate_exp"], 1)

            def expert_round(r):
                stage, _ = stage_release(expert_jobs, lambda j: ("egu", r, j), ("ey", r, 1))

                def silu(e, j):
                    wait_filled(act, "egu", r, j, e=e)
                    nc.scalar.activation(sg[:, j % 2], bank(("egu", r, j))[:, 0:256], ACT.Silu).then_inc(s["sg_ready"], 1)

                def hidden(e, j):
                    wait_filled(act, "ehT", r, j, e=e)
                    nc.scalar.copy(h_hi[:, j % 2, :, 0:P],
                                   bank(("ehT", r, j))[:, 0:256].rearrange("p (k s) -> p k s", k=2)).then_inc(s["hT_hi"], 1)

                def hi_block(e, i):
                    sl = (BASE + i) % SLOTS
                    act.wait_ge(landed[sl], e * e_total[sl] + (e_landed[i] + r * NE * e_total[sl]))
                    stage_free(act, stage[(i - STAGES) % JOBS_E], e if i >= STAGES else e - 1, r)
                    nc.scalar.copy(w_hi[:, i % STAGES, :], slot_of(BASE + i)).then_inc(s["hi_ready"], 1)

                def scatter_matrix(e, _):
                    b, n = uses["eo", r, 3]
                    act.wait_ge(bank_filled[b], e * per_expert[b] + (n + 1 - per_expert[b]))
                    nc.scalar.copy(sc_cur, scT[:, bass.ds(e * 256, 256)]).then_inc(s["sc_ready"], 1)

                def result(e, n_):
                    wait_filled(act, "ey", r, n_, e=e)
                    free(nc.scalar.copy(ye[:, 512 * n_:512 * n_ + 512], bank(("ey", r, n_))), "ey", r, n_)

                def gathered(e, _):
                    act.wait_ge(s["xg_raw"], e * 2 + (2 + 2 * NE * r))
                    nc.scalar.copy(x_hi[:, :, 0:P], xg).then_inc(s["xT_hi"], 1)

                do = {"block": hi_block, "silu": silu, "hidden": hidden, "scatter_matrix": scatter_matrix,
                      "result": result, "gathered": gathered}
                for i in range(HI_AHEAD):
                    hi_block(0, i)
                gathered(0, 0)
                for i in range(4):
                    wait_filled(act, "scT", r, i)
                    free(nc.scalar.copy(scT[:, 512 * i:512 * i + 512], bank(("scT", r, i))), "scT", r, i)
                for i in range(4):
                    wait_taken(act, "scT", r, i)
                experts(act, SCALAR_EXPERT, do, HI_AHEAD)

            expert_round(0)
            act.wait_ge(s["flag_ready"], 1)
            more = act.value_load(flag[0:1, 0:1], min_val=0, max_val=1)
            with act.If(more):
                expert_round(1)
            act.dma_start(fin_w, a["final_norm_w"].rearrange("(o d) -> o d", o=1).to_broadcast([P, D])).then_inc(finw_in, 16)
            act.wait_ge(s["h_final"], 1)
            row_norm(h)

        @block.vector
        def _(dve):
            ch = Chain(dve, dve_step)
            v = nc.vector

            def tt(out_, x, y, op):
                ch.do(v.tensor_tensor(out_, x, y, op))

            nc.vector.memset(eps[:, 0:1], EPS).then_inc(s["eps_ready"], 1)
            ch.do(v.memset(stat[:, 60:64], 0.0))

            norm_no = [0]

            def scale_rows(src):
                n = norm_no[0]
                norm_no[0] += 1
                dve.wait_ge(s["rstd_ready"], n + 1)
                for t in range(TT):
                    ins = v.tensor_scalar(hs[:, t, :], src[:, t, :], stat[:, 4 * n + t:4 * n + t + 1], None, ALU.mult)
                    if t == TT - 1:
                        ins.then_inc(s["hs_ready"], 1)
                    else:
                        ch.do(ins)
                ch.settle()

            def scaled_transposes(l, which, dst, weight, wl):
                for i in range(4):
                    wait_filled(dve, "normT", l, which, i)
                    w = cols[:, ROW[weight, wl] + 2 * i:ROW[weight, wl] + 2 * i + 2]
                    free(v.tensor_tensor(dst[:, 2 * i:2 * i + 2, :], bank(("normT", l, which, i)).rearrange("p (c s) -> p c s", c=2),
                                         w.rearrange("p (c o) -> p c o", o=1).to_broadcast([P, 2, 256]), ALU.mult), "normT", l, which, i)

            scale_rows(h)
            wait_filled(dve, "cols")
            free(v.tensor_copy(cols[:, :], bank(("cols",))[:, 0:P + DEPTH * NT]), "cols")
            wait_taken(dve, "cols")
            scaled_transposes(0, "mix", xT, "mix_norm", 0)
            dve.wait_ge(s["sp_dt"], 1)
            lam = cols[:, 0:32].rearrange("p (l q i) -> p l q i", l=2, q=2)

            def spv(i):
                return sp[:, i, :].rearrange("p (l i) -> p l i", l=2)

            tt(spv(2), lam[:, :, 0, :], spv(1), ALU.mult)
            tt(spv(8), lam[:, :, 1, :], spv(1), ALU.mult)
            ch.settle()
            ch.do(v.tensor_scalar(sp[:, 9, :], sp[:, 8, :], 1.0 / (2 * math.pi), None, ALU.mult))
            ch.settle()
            ch.do(v.tensor_scalar(sp[:, 10, :], sp[:, 9, :], ROUNDER, None, ALU.add))
            ch.settle()
            ch.do(v.tensor_scalar(sp[:, 9, :], sp[:, 10, :], ROUNDER, None, ALU.subtract))
            ch.settle()
            ch.do(v.scalar_tensor_tensor(out=sp[:, 10, :], in0=sp[:, 9, :], scalar=-TWO_PI_HI, in1=sp[:, 8, :], op0=ALU.mult, op1=ALU.add))
            ch.settle()
            ch.do(v.scalar_tensor_tensor(out=sp[:, 11, :], in0=sp[:, 9, :], scalar=-TWO_PI_LO, in1=sp[:, 10, :], op0=ALU.mult, op1=ALU.add))
            ch.settle()
            v.tensor_scalar(sp[:, 3, :], sp[:, 11, :], 3.1415925, -3.1415925, ALU.min, ALU.max).then_inc(s["sp_range"], 1)
            dve.wait_ge(s["sp_sin"], 1)
            tt(sp[:, 8, :], sp[:, 6, :], sp[:, 7, :], ALU.mult)
            ch.settle()
            ch.do(v.tensor_scalar(sp[:, 12, :], sp[:, 8, :], -2.0, 1.0, ALU.mult, ALU.add))
            ch.settle()
            tt(sp[:, 13, :], sp[:, 12, :], sp[:, 4, :], ALU.mult)
            tt(sp[:, 14, :], sp[:, 5, :], sp[:, 4, :], ALU.mult)
            tt(spv(15), lam[:, :, 0, :], lam[:, :, 0, :], ALU.mult)
            tt(spv(16), lam[:, :, 1, :], lam[:, :, 1, :], ALU.mult)
            ch.settle()
            tt(sp[:, 17, :], sp[:, 15, :], sp[:, 16, :], ALU.add)
            ch.do(v.tensor_scalar(sp[:, 13, :], sp[:, 13, :], -1.0, None, ALU.add))
            ch.settle()
            ch.do(v.reciprocal(sp[:, 18, :], sp[:, 17, :]))
            tt(spv(15), spv(13), lam[:, :, 0, :], ALU.mult)
            tt(spv(16), spv(14), lam[:, :, 1, :], ALU.mult)
            tt(spv(17), spv(14), lam[:, :, 0, :], ALU.mult)
            tt(spv(19), spv(13), lam[:, :, 1, :], ALU.mult)
            ch.settle()
            tt(sp[:, 15, :], sp[:, 15, :], sp[:, 16, :], ALU.add)
            tt(sp[:, 17, :], sp[:, 17, :], sp[:, 19, :], ALU.subtract)
            ch.settle()
            tt(sp[:, 8, :], sp[:, 15, :], sp[:, 18, :], ALU.mult)
            v.tensor_tensor(sp[:, 9, :], sp[:, 17, :], sp[:, 18, :], ALU.mult).then_inc(s["sp_ready"], 1)
            ch.settle()
            dve.wait_ge(consts_in, 16)
            scale_rows(memT.rearrange("p (t c) s -> p t (c s)", t=TT))
            dve.wait_ge(s["hs_ready"], 2)
            scaled_transposes("mem", 0, memT, "mem_norm", 0)

            def add_to_h(keys):
                for key, t, n in keys:
                    wait_filled(dve, *key)
                    hv = h[:, t, 512 * n:512 * n + 512]
                    free(v.tensor_tensor(hv, hv, bank(key), ALU.add), *key)
                for key, t, n in keys:
                    wait_taken(dve, *key)

            for l in range(DEPTH):
                if l:
                    scale_rows(h)
                    scaled_transposes(l, "mix", xT, "mix_norm", l)
                cos = c("rope_cos").rearrange("p (t q o f) -> p t q o f", t=2, q=2, o=1)
                sin = c("rope_sin").rearrange("p (t q o f) -> p t q o f", t=2, q=2, o=1)
                for t in range(TT):
                    wait_filled(dve, "rqk", l, t)
                    src = bank(("rqk", l, t)).rearrange("p (q h x f) -> p q h x f", q=2, h=RH, x=2)
                    dst = rqk[:, t, :].rearrange("p (q h x f) -> p q h x f", q=2, h=RH, x=2)
                    t1 = rtmp[:, 0].rearrange("p (q h f) -> p q h f", q=2, h=RH)
                    t2 = rtmp[:, 1].rearrange("p (q h f) -> p q h f", q=2, h=RH)
                    cb_ = cos[:, t].to_broadcast([P, 2, RH, 32])
                    sb_ = sin[:, t].to_broadcast([P, 2, RH, 32])
                    tt(t1, src[:, :, :, 0, :], cb_, ALU.mult)
                    tt(t2, src[:, :, :, 1, :], sb_, ALU.mult)
                    ch.settle()
                    tt(dst[:, :, :, 0, :], t1, t2, ALU.subtract)
                    ch.settle()
                    tt(t1, src[:, :, :, 0, :], sb_, ALU.mult)
                    free(v.tensor_tensor(t2, src[:, :, :, 1, :], cb_, ALU.mult), "rqk", l, t)
                    ch.settle()
                    wait_taken(dve, "rqk", l, t)
                    ins = v.tensor_tensor(dst[:, :, :, 1, :], t1, t2, ALU.add)
                    if t == TT - 1:
                        ins.then_inc(s["rqk_ready"], 1)
                    else:
                        ch.do(ins)
                        ch.settle()
                wait_filled(dve, "BT", l)
                free(v.tensor_copy(BT.rearrange("p f r s -> p (f r s)"), bank(("BT", l))), "BT", l)
                wait_filled(dve, "CT", l)
                cb4 = bank(("CT", l)).rearrange("p (f r s) -> p f r s", f=2, r=2)
                gm = c("group_mask").rearrange("p (o s) -> p o s", o=1).to_broadcast([P, 2, P])
                ch.do(v.tensor_tensor(CT[:, :, 0, :], cb4[:, :, 0, :], gm, ALU.mult))
                ch.settle()
                free(v.scalar_tensor_tensor(out=CT[:, :, 1, :], in0=cb4[:, :, 1, :], scalar=-1.0, in1=gm, op0=ALU.mult, op1=ALU.mult), "CT", l)

                dve.wait_ge(s["rot_ready"], l + 1)
                for g in range(4):
                    wait_taken(dve, "bu", l, 2 * g)
                    wait_taken(dve, "bu", l, 2 * g + 1)
                    if l or g:
                        dve.wait_ge(s["x_im"], 4 * l + g)
                    pre, pim = rot_tab[:, 0, 2 * g:2 * g + 2, :], rot_tab[:, 1, 2 * g:2 * g + 2, :]
                    bre, bim = zone_b[:, 2 * g:2 * g + 2, 0, :], zone_b[:, 2 * g:2 * g + 2, 1, :]
                    tt(yin[:, 0], pre, bre, ALU.mult)
                    tt(vtmp, pim, bim, ALU.mult)
                    ch.settle()
                    tt(yin[:, 0], yin[:, 0], vtmp, ALU.add)
                    ch.settle()
                    for r in range(2):
                        if r == 1:
                            dve.wait_ge(s["yin_im"], 4 * l + g + 1)
                        for i in range(2):
                            mag = sp[:, 4, 8 * l + 2 * g + i:8 * l + 2 * g + i + 1]
                            ins = v.tensor_tensor_scan(ysc[:, r, i, :], mag.to_broadcast([P, S]), yin[:, r, i, :], 0.0, ALU.mult, ALU.add)
                            if r and i:
                                ins.then_inc(s["ysc_ready"], 1)
                            else:
                                ch.do(ins)
                    ch.settle()
                    dve.wait_ge(s["ysc_ready"], 4 * l + g + 1)
                    tt(bre, pre, ysc[:, 0], ALU.mult)
                    tt(vtmp, pim, ysc[:, 1], ALU.mult)
                    ch.settle()
                    v.tensor_tensor(bre, bre, vtmp, ALU.subtract).then_inc(s["x_re"], 1)
                dve.wait_ge(s["x_re"], 4 * l + 4)

                dec = c("decay").rearrange("p (h s) -> p h s", h=RH)
                for hd in range(RH):
                    wait_filled(dve, "rs", l, hd)
                    bk = bank(("rs", l, hd))
                    ch.do(v.tensor_tensor(rsc[:, hd % 2, 0:256], bk[:, 0:256], dec[:, hd, :], ALU.mult))
                    ch.settle()
                    free(v.tensor_tensor(rsc[:, hd % 2, 256:384], bk[:, 256:384], dec[:, hd, 0:P], ALU.mult), "rs", l, hd)
                wait_filled(dve, "ro", l)
                ob = bank(("ro", l)).rearrange("p (g f) -> p g f", g=8)
                rog = ro.rearrange("p t (h f) -> p (t h) f", h=RH)
                ro2g = ro2.rearrange("p t (h f) -> p (t h) f", h=RH)
                mu, dev = stat[:, 32:40], stat[:, 48:56]

                def wide(x):
                    return x.rearrange("p (g o) -> p g o", o=1).to_broadcast([P, 8, DH])

                ch.do(v.tensor_reduce(mu, ob, AX_X, ALU.add))
                ch.settle()
                ch.do(v.tensor_scalar(mu, mu, 1.0 / DH, None, ALU.mult))
                ch.settle()
                free(v.tensor_tensor(rog, ob, wide(mu), ALU.subtract), "ro", l)
                wait_taken(dve, "ro", l)
                tt(ro2g, rog, rog, ALU.mult)
                ch.settle()
                v.tensor_reduce(mu, ro2g, AX_X, ALU.add).then_inc(s["rgn_sq"], 1)
                dve.wait_ge(s["rgn_rstd"], l + 1)
                tt(rog, rog, wide(dev), ALU.mult)
                ch.settle()
                v.tensor_tensor(ro, ro, rvg[:, :, 256:512], ALU.mult).then_inc(s["yb_ready"], 1)

                for step in range(SH + 1):
                    if step < SH:
                        hd = step
                        dve.wait_ge(s["sa_ready"], SH * l + hd + 1)
                        lf = slf[:, hd % 2]
                        free(v.scalar_tensor_tensor(out=lf, in0=bank(("sz", l, hd))[:, 0:384], scalar=0.0, in1=sa[:, hd % 2],
                                                    op0=ALU.max, op1=ALU.add), "sz", l, hd)
                        wait_taken(dve, "sz", l, hd)
                        v.tensor_tensor(lf, lf, c("neg_mask"), ALU.mult).then_inc(s["slf_ready"], 1)
                    if step >= 1:
                        hd = step - 1
                        wait_filled(dve, "sc", l, hd)
                        free(v.scalar_tensor_tensor(out=sw[:, hd % 2], in0=bank(("sc", l, hd))[:, 0:384], scalar=0.0,
                                                    in1=c("mask_bias"), op0=ALU.min, op1=ALU.add), "sc", l, hd)
                    if step - 1 in FILLERS:
                        i = FILLERS.index(step - 1)
                        dve.wait_ge(s["yb_ready"], l + 1)
                        wait_filled(dve, "kT", l, i)
                        free(v.tensor_copy(kT[:, 2 * i:2 * i + 2, :].rearrange("p c s -> p (c s)"), bank(("kT", l, i))), "kT", l, i)

                wait_filled(dve, "ybT", l)
                g2 = cols[:, ROW["gain", l] + 2:ROW["gain", l] + 4]
                free(v.tensor_tensor(yT[:, 2:4, :], bank(("ybT", l)).rearrange("p (c s) -> p c s", c=2),
                                     g2.rearrange("p (c o) -> p c o", o=1).to_broadcast([P, 2, 256]), ALU.mult), "ybT", l)
                wait_filled(dve, "y", l)
                for cc in range(2):
                    ins = v.scalar_tensor_tensor(out=glu_s[:, cc, :], in0=uT[:, cc, :], scalar=col("ssm_d", l, cc),
                                                 in1=bank(("y", l))[:, 256 * cc:256 * cc + 256], op0=ALU.mult, op1=ALU.add)
                    if cc:
                        free(ins, "y", l)
                    else:
                        ch.do(ins)
                        ch.settle()
                wait_taken(dve, "glu", l)
                v.tensor_tensor(gT, gT, glu_s, ALU.mult).then_inc(s["glu_ready"], 1)
                dve.wait_ge(s["glu_ready"], l + 1)
                dve.wait_ge(s["rstda"], l + 1)
                for cc in range(2):
                    ins = v.scalar_tensor_tensor(out=yT[:, cc, :], in0=gT[:, cc, :], scalar=col("gain", l, cc), in1=rstd_a,
                                                 op0=ALU.mult, op1=ALU.mult)
                    ch.do(ins)
                ch.settle()
                v.tensor_copy(stat[:, 60:61], stat[:, 62:63]).then_inc(s["ya_T"], 1)
                dve.wait_ge(s["rstdc"], l + 1)
                for cc in range(4):
                    ch.do(v.scalar_tensor_tensor(out=yT[:, 4 + cc, :], in0=yT[:, 4 + cc, :], scalar=col("gain", l, 4 + cc), in1=rstd_c,
                                                 op0=ALU.mult, op1=ALU.mult))
                ch.settle()
                v.tensor_copy(stat[:, 60:61], stat[:, 62:63]).then_inc(s["yc_T"], 1)
                def attn_w_lo(m):
                    w, w_rest = attn_pair(m)
                    dve.wait_ge(s["attn_w_hi"], m + 1)
                    v.tensor_tensor(w_rest, slot_of(job_no[attn_jobs[m]]), w.bitcast(F32), ALU.subtract).then_inc(s["attn_w_lo"], 1)

                q0, o0 = 16 * l, 16 * l + 8
                add_to_h([(("out", l, 0, t), t, 0) for t in range(TT)])
                attn_w_lo(q0)
                attn_w_lo(q0 + 1)
                add_to_h([(("out", l, 1, t), t, 1) for t in range(TT)])

                scale_rows(h)
                scaled_transposes(l, "cross", xT, "cross_norm", l)
                for i in range(4):
                    ks = slice(2 * i, 2 * i + 2)
                    dve.wait_ge(s["attn_x_hi"], 8 * l + i + 1)
                    v.tensor_tensor(x_lo[:, ks, :], xT[:, ks, :], x_hi[:, ks, :].bitcast(F32), ALU.subtract).then_inc(s["attn_x_lo"], 1)
                for m in range(2, 8):
                    attn_w_lo(q0 + m)

                def head_out(hd):
                    n = 8 * l + 4 + hd + 1
                    dve.wait_ge(s["attn_x_hi"], n)
                    v.tensor_tensor(y_lo[:, 2 * hd:2 * hd + 2, :].rearrange("p c s -> p (c s)"), bank(("co", l, hd)),
                                    x_hi[:, 2 * hd:2 * hd + 2, :].rearrange("p c s -> p (c s)").bitcast(F32),
                                    ALU.subtract).then_inc(s["attn_x_lo"], 1)
                    dve.wait_ge(s["attn_x_lo"], n)
                    free(v.tensor_copy(stat[:, 60:61], stat[:, 62:63]), "co", l, hd)

                for hd in range(CH):
                    wait_filled(dve, "cs", l, hd)
                    ch.do(v.tensor_reduce(cstat[:, 0:2], bank(("cs", l, hd)).rearrange("p (t s) -> p t s", t=2), AX_X, ALU.max))
                    ch.settle()
                    v.tensor_scalar(stat[:, 56:58], cstat[:, 0:2], -1.0, None, ALU.mult).then_inc(s["cs_max"], 1)
                    dve.wait_ge(s["cp_exp"], CH * l + hd + 1)
                    free(v.reciprocal(cstat[:, 2:4], stat[:, 58:60]), "cs", l, hd)
                    wait_taken(dve, "cs", l, hd)
                    for t in range(TT):
                        ins = v.tensor_scalar(cp[:, hd % 2, t, :], cp[:, hd % 2, t, :], cstat[:, 2 + t:3 + t], None, ALU.mult)
                        if t:
                            ins.then_inc(s["cp_ready"], 1)
                        else:
                            ch.do(ins)
                            ch.settle()
                    if hd:
                        head_out(hd - 1)
                    if hd >= 2:
                        attn_w_lo(o0 + hd - 2)
                head_out(CH - 1)
                for m in range(2, 7):
                    attn_w_lo(o0 + m)
                add_to_h([(("o", l, 0, t), t, 0) for t in range(TT)])
                attn_w_lo(o0 + 7)
                add_to_h([(("o", l, 1, t), t, 1) for t in range(TT)])

                scale_rows(h)
                if l:
                    scaled_transposes(l, "ffn", xT, "ffn_norm", l)
                else:
                    def gated(j):
                        for t in range(TT):
                            dve.wait_ge(s["sg_ready"], 2 * j + t + 1)
                            if j >= 2:
                                wait_filled(dve, "hT", j - 2, t)
                            free(v.tensor_tensor(hh[:, j % 2, t, :], sg[:, t], bank(("gu", j, t))[:, 256:512], ALU.mult), "gu", j, t)

                    def hidden(j):
                        for t in range(TT):
                            dve.wait_ge(s["hT_hi"], 2 * j + t + 1)
                            ts = slice(t * P, (t + 1) * P)
                            v.tensor_tensor(h_lo[:, j % 2, :, ts], bank(("hT", j, t))[:, 0:256].rearrange("p (k s) -> p k s", k=2),
                                            h_hi[:, j % 2, :, ts].bitcast(F32), ALU.subtract).then_inc(s["hT_lo"], 1)
                            dve.wait_ge(s["hT_lo"], 2 * j + t + 1)
                            free(v.tensor_copy(stat[:, 60:61], stat[:, 62:63]), "hT", j, t)

                    def lo_block(i):
                        dve.wait_ge(s["hi_ready"], i + 1)
                        v.tensor_tensor(w_lo[:, i % STAGES, :], slot_of(job_no[dense_jobs[i]]), w_hi[:, i % STAGES, :].bitcast(F32),
                                        ALU.subtract).then_inc(s["lo_ready"], 1)

                    for i in range(LO_AHEAD):
                        lo_block(i)
                    scaled_transposes(l, "ffn", xT, "ffn_norm", l)
                    for i in range(4):
                        ks = slice(2 * i, 2 * i + 2)
                        dve.wait_ge(s["xT_hi"], i + 1)
                        v.tensor_tensor(x_lo[:, ks, :], xT[:, ks, :], x_hi[:, ks, :].bitcast(F32), ALU.subtract).then_inc(s["xT_lo"], 1)
                    dve.wait_ge(s["xT_lo"], 4)
                    for _, what, j in schedule(VECTOR_DENSE):
                        if what != "block" or j >= LO_AHEAD:
                            {"block": lo_block, "gated": gated, "hidden": hidden}[what](j)
                    add_to_h([(("down", 2 * t + n), t, n) for t in range(TT) for n in range(2)])

            def r3(i):
                return rt[:, i, :].rearrange("p (t e) -> p t e", t=2)

            def over_e(x):
                return x.rearrange("p (t o) -> p t o", o=1).to_broadcast([P, 2, NE])

            MASK, DIFF, EXPD, LOG, EQ, KEY, OH1, OH2, GATE, SLOTN, MX, CNT = range(12)
            key8 = c("first_key").rearrange("p (o e) -> p o e", o=1).to_broadcast([P, 2, NE])
            wait_filled(dve, "logits")
            free(v.tensor_copy(rt[:, LOG, :], bank(("logits",))[:, 0:16]), "logits")
            wait_taken(dve, "logits")
            for k, oh in enumerate((OH1, OH2)):
                m = rt[:, MX, 4 * k:4 * k + 2]
                ch.do(v.tensor_reduce(m, r3(LOG), AX_X, ALU.max))
                ch.settle()
                tt(r3(EQ), r3(LOG), over_e(m), ALU.is_equal)
                ch.settle()
                tt(r3(KEY), r3(EQ), key8, ALU.mult)
                ch.settle()
                ch.do(v.tensor_reduce(rt[:, MX, 4 * k + 2:4 * k + 4], r3(KEY), AX_X, ALU.max))
                ch.settle()
                tt(r3(oh), r3(KEY), over_e(rt[:, MX, 4 * k + 2:4 * k + 4]), ALU.is_equal)
                ch.settle()
                if k == 0:
                    ch.do(v.scalar_tensor_tensor(out=rt[:, LOG, :], in0=rt[:, OH1, :], scalar=-1e30, in1=rt[:, LOG, :],
                                                 op0=ALU.mult, op1=ALU.add))
                    ch.settle()
            v.tensor_tensor(rt[:, MASK, :], rt[:, OH1, :], rt[:, OH2, :], ALU.add).then_inc(s["mask_ready"], 1)
            v.tensor_tensor(rt[:, DIFF, 0:2], rt[:, MX, 4:6], rt[:, MX, 0:2], ALU.subtract).then_inc(s["gate_in"], 1)
            dve.wait_ge(s["gate_exp"], 1)
            ch.do(v.tensor_scalar(rt[:, EXPD, 2:4], rt[:, EXPD, 0:2], 1.0, None, ALU.add))
            ch.settle()
            ch.do(v.reciprocal(rt[:, EXPD, 4:6], rt[:, EXPD, 2:4]))
            ch.settle()
            tt(rt[:, EXPD, 6:8], rt[:, EXPD, 4:6], rt[:, EXPD, 0:2], ALU.mult)
            tt(r3(OH1), r3(OH1), over_e(rt[:, EXPD, 4:6]), ALU.mult)
            ch.settle()
            tt(r3(OH2), r3(OH2), over_e(rt[:, EXPD, 6:8]), ALU.mult)
            ch.settle()
            tt(rt[:, GATE, :], rt[:, OH1, :], rt[:, OH2, :], ALU.add)
            ch.settle()
            wait_filled(dve, "rank")
            rk = bank(("rank",))
            ch.do(v.tensor_reduce(rt[:, CNT, 0:1], rk[:, 16:24], AX_X, ALU.max))
            free(v.scalar_tensor_tensor(out=rt[:, SLOTN, :], in0=rk[:, 0:16], scalar=1.0, in1=rt[:, MASK, :], op0=ALU.add, op1=ALU.mult), "rank")
            ch.settle()
            wait_taken(dve, "rank")
            v.tensor_scalar(flag[:, :], rt[:, CNT, 0:1], float(ROUND) + 0.5, None, ALU.is_ge).then_inc(s["flag_ready"], 1)

            def expert_round(r):
                if r:
                    wait_filled(dve, "eo", 0, 3, e=NE - 1)
                ch.do(v.tensor_scalar(rt[:, EQ, :], rt[:, SLOTN, :], -1.0 - r * ROUND, None, ALU.add))
                ch.settle()

                def spread(x):
                    return x.rearrange("p (t e o) -> p e t o", t=2, o=1).to_broadcast([P, NE, 2, P])

                io = c("iota").rearrange("p (a b s) -> p a b s", a=1, b=1).to_broadcast([P, NE, 2, P])
                sel4 = sel.rearrange("p (e t s) -> p e t s", e=NE, t=2)
                gsel4 = gsel[:, :].rearrange("p (e t s) -> p e t s", e=NE, t=2)
                v.tensor_tensor(sel4, spread(rt[:, EQ, :]), io, ALU.is_equal).then_inc(s["sel_ready"], 1)
                dve.wait_ge(s["sel_ready"], r + 1)
                v.tensor_tensor(gsel4, sel4, spread(rt[:, GATE, :]), ALU.mult).then_inc(s["gsel_ready"], 1)
                fw = cols[:, ROW["ffn_norm", 1]:ROW["ffn_norm", 1] + 8].rearrange("p (c o) -> p c o", o=1)

                def tokens(e, _):
                    for i in range(2):
                        wait_filled(dve, "xg", r, i, e=e)
                        v.tensor_tensor(xg[:, 4 * i:4 * i + 4, :], bank(("xg", r, i)).rearrange("p (c s) -> p c s", c=4),
                                        fw[:, 4 * i:4 * i + 4].to_broadcast([P, 4, P]), ALU.mult).then_inc(s["xg_raw"], 1)

                def tokens_rest(e, _):
                    dve.wait_ge(s["xT_hi"], e + (5 + NE * r))
                    for i in range(2):
                        dve.wait_ge(s["xg_raw"], e * 2 + (2 + 2 * NE * r))
                        free(v.tensor_copy(stat[:, 56 + i:57 + i], stat[:, 62:63]), "xg", r, i)
                    v.tensor_tensor(x_lo[:, :, 0:P], xg, x_hi[:, :, 0:P].bitcast(F32), ALU.subtract).then_inc(s["xT_lo"], 1)

                def gated(e, j):
                    dve.wait_ge(s["sg_ready"], e * NJ + (2 * NJ + j + 1 + r * NE * NJ))
                    if j >= 2:
                        wait_filled(dve, "ehT", r, j - 2, e=e)
                    free(v.tensor_tensor(hh[:, j % 2, 0, :], sg[:, j % 2], bank(("egu", r, j))[:, 256:512], ALU.mult), "egu", r, j)

                def hidden(e, j):
                    n = e * NJ + (2 * NJ + j + 1 + r * NE * NJ)
                    dve.wait_ge(s["hT_hi"], n)
                    v.tensor_tensor(h_lo[:, j % 2, :, 0:P], bank(("ehT", r, j))[:, 0:256].rearrange("p (k s) -> p k s", k=2),
                                    h_hi[:, j % 2, :, 0:P].bitcast(F32), ALU.subtract).then_inc(s["hT_lo"], 1)
                    dve.wait_ge(s["hT_lo"], n)
                    free(v.tensor_copy(stat[:, 60:61], stat[:, 62:63]), "ehT", r, j)

                def lo_block(e, i):
                    dve.wait_ge(s["hi_ready"], e * JOBS_E + (JOBS_E * (1 + NE * r) + i + 1))
                    v.tensor_tensor(w_lo[:, i % STAGES, :], slot_of(BASE + i), w_hi[:, i % STAGES, :].bitcast(F32),
                                    ALU.subtract).then_inc(s["lo_ready"], 1)

                def scattered(e, i):
                    wait_filled(dve, "eo", r, i, e=e)
                    hv = h[:, i // 2, 512 * (i % 2):512 * (i % 2) + 512]
                    free(v.tensor_tensor(hv, hv, bank(("eo", r, i)), ALU.add), "eo", r, i)

                do = {"block": lo_block, "gated": gated, "hidden": hidden, "tokens": tokens, "tokens_rest": tokens_rest,
                      "scattered": scattered}
                for i in range(LO_AHEAD):
                    lo_block(0, i)
                tokens(0, 0)
                tokens_rest(0, 0)
                experts(dve, VECTOR_EXPERT, do, LO_AHEAD)

            expert_round(0)
            dve.wait_ge(s["flag_ready"], 1)
            more = dve.value_load(flag[0:1, 0:1], min_val=0, max_val=1)
            with dve.If(more):
                expert_round(1)
            v.tensor_copy(stat[:, 60:61], stat[:, 62:63]).then_inc(s["h_final"], 1)
            n = norm_no[0]
            dve.wait_ge(s["rstd_ready"], n + 1)
            dve.wait_ge(finw_in, 16)
            for t in range(TT):
                v.scalar_tensor_tensor(out=hs[:, t, :], in0=h[:, t, :], scalar=stat[:, 4 * n + t:4 * n + t + 1], in1=fin_w,
                                       op0=ALU.mult, op1=ALU.mult).then_inc(s["final_ready"], 1)

        @block.gpsimd
        def _(pool):
            ch = Chain(pool, pool_step)
            g_ = nc.gpsimd

            def tt(out_, x, y, op):
                ch.do(g_.tensor_tensor(out_, x, y, op))

            
            pool.wait_ge(s["sp_ready"], 1)
            for l in range(DEPTH):
                pool.wait_ge(ssm_in, 16 * N_SSM_LOADS * (l + 1))
                if l:
                    wait_filled(pool, "gu", 0, 0)
                ch.do(g_.memset(bb[:, :, :, :], 0.0))
                ch.settle()
                for q in range(2):
                    p0 = 64 * q
                    rows = slice(p0, p0 + 64)

                    def z(i):
                        return sp[rows, i, 8 * l:8 * l + 8].rearrange("p (i o) -> p i o", o=1).to_broadcast([64, NT, 16])

                    br, bi = braw[rows, 0], braw[rows, 1]
                    for r, (x, y, op) in enumerate(((br, bi, ALU.subtract), (bi, br, ALU.add))):
                        tt(bbt[rows, 0], z(8), x, ALU.mult)
                        tt(bbt[rows, 1], z(9), y, ALU.mult)
                        ch.settle()
                        ins = g_.tensor_tensor(bb[rows, r, :, 16 * q:16 * q + 16], bbt[rows, 0], bbt[rows, 1], op)
                        if q and r:
                            ins.then_inc(s["bb_ready"], 1)
                        else:
                            ch.do(ins)
                            ch.settle()
                pool.wait_ge(s["bb_ready"], l + 1)
                re, im = rot_tab[:, 0], rot_tab[:, 1]
                ch.do(g_.memset(re[:, :, 0:1], 1.0))
                ch.do(g_.memset(im[:, :, 0:1], 0.0))
                ch.do(g_.tensor_copy(re[:, :, 1:2], sp[:, 12, 8 * l:8 * l + 8].rearrange("p (i o) -> p i o", o=1)))
                ch.do(g_.tensor_copy(im[:, :, 1:2], sp[:, 5, 8 * l:8 * l + 8].rearrange("p (i o) -> p i o", o=1)))
                ch.settle()
                m = 1
                while m < S:
                    n = min(m, S - 1 - m)
                    if n <= 0:
                        break
                    w_ = [P, NT, n]
                    lo, hi, top = slice(1, n + 1), slice(m + 1, m + n + 1), slice(m, m + 1)
                    t1 = rot_tmps[l][:, 0, :, 0:n]
                    t2 = rot_tmps[l][:, 1, :, 0:n]
                    mr, mi = re[:, :, top].to_broadcast(w_), im[:, :, top].to_broadcast(w_)
                    tt(t1, re[:, :, lo], mr, ALU.mult)
                    tt(t2, im[:, :, lo], mi, ALU.mult)
                    ch.settle()
                    tt(re[:, :, hi], t1, t2, ALU.subtract)
                    ch.settle()
                    tt(t1, re[:, :, lo], mi, ALU.mult)
                    tt(t2, im[:, :, lo], mr, ALU.mult)
                    ch.settle()
                    tt(im[:, :, hi], t1, t2, ALU.add)
                    ch.settle()
                    m *= 2
                g_.memset(ptmp[:, 0, 0:1], 0.0).then_inc(s["rot_ready"], 1)
                pool.wait_ge(s["rot_ready"], l + 1)
                for g in range(4):
                    wait_taken(pool, "bu", l, 2 * g)
                    wait_taken(pool, "bu", l, 2 * g + 1)
                    pre, pim = rot_tab[:, 0, 2 * g:2 * g + 2, :], rot_tab[:, 1, 2 * g:2 * g + 2, :]
                    bre, bim = zone_b[:, 2 * g:2 * g + 2, 0, :], zone_b[:, 2 * g:2 * g + 2, 1, :]
                    if g:
                        pool.wait_ge(s["x_im"], 4 * l + g)
                    if l or g:
                        pool.wait_ge(s["ysc_ready"], 4 * l + g)
                    tt(yin[:, 1], pre, bim, ALU.mult)
                    tt(ptmp[:, :, :], pim, bre, ALU.mult)
                    ch.settle()
                    g_.tensor_tensor(yin[:, 1], yin[:, 1], ptmp[:, :, :], ALU.subtract).then_inc(s["yin_im"], 1)
                    pool.wait_ge(s["yin_im"], 4 * l + g + 1)
                    pool.wait_ge(s["ysc_ready"], 4 * l + g + 1)
                    tt(bim, pre, ysc[:, 1], ALU.mult)
                    tt(ptmp[:, :, :], pim, ysc[:, 0], ALU.mult)
                    ch.settle()
                    g_.tensor_tensor(bim, bim, ptmp[:, :, :], ALU.add).then_inc(s["x_im"], 1)

_INS = ["x", "mem", "mix_norm_w", "w_in", "ssm_lambda_re", "ssm_lambda_im", "ssm_b_re", "ssm_b_im", "ssm_c_re", "ssm_c_im",
        "ssm_d", "ssm_log_dt", "ssm_w_glu", "mix_out_gain", "w_out", "cross_norm_w", "mem_norm_w", "w_cross_q", "w_cross_kv",
        "w_cross_o", "ffn_norm_w", "w_dense_gu", "w_dense_down", "w_router", "w_expert_gu", "w_expert_down", "final_norm_w"]


def kernel(**inputs):
    import concourse.bacc as _bacc
    from concourse.bass_utils import run_bass_kernel_spmd as _run

    nc = _bacc.Bacc("TRN2", target_bir_lowering=False, num_devices=1, dynamic_dma_scratch_size=1024)
    arrays, args = {}, {}
    host = {n: np.ascontiguousarray(inputs[n]) for n in _INS}
    host["consts"] = constants()
    for name, v in host.items():
        arrays[f"in_{name}"] = v
        args[name] = nc.dram_tensor(f"in_{name}", v.shape, mybir.dt.from_np(v.dtype), kind="ExternalInput").ap()
    out = nc.dram_tensor("out_0", (1, S, D), F32, kind="ExternalOutput").ap()
    trunk(nc, args, out)
    r = _run(nc, [arrays], core_ids=[0])
    return r.results[0]["out_0"]
```
